# Optimizing a Trainium2 kernel written in Bass

```python
import math
import jax
import jax.numpy as jnp
from jax import lax
import numpy as np

D_MODEL = 1024
BATCH = 1
SEQ = 1024
DEPTH = 1

CHUNK = 64
EPS = 1e-6
A_HEADS = 8
A_HEAD_DIM = 64
A_WIDTH = A_HEADS * A_HEAD_DIM
A_PAST_CHUNKS = 8
A_BAND = A_PAST_CHUNKS + 1
A_MAX_REL = 128
B_HEADS = 4
B_HEAD_DIM = 128
B_WIDTH = B_HEADS * B_HEAD_DIM
CONV_K = 4
FFN_HIDDEN = ((8 * D_MODEL + 3 * 256 - 1) // (3 * 256)) * 256
N_MOD = 6
IN_SIZES = (A_WIDTH, A_WIDTH, A_WIDTH, 3 * B_WIDTH, B_WIDTH, B_HEADS, B_HEADS, D_MODEL, D_MODEL)
IN_DIM = sum(IN_SIZES)
IN_SPLITS = tuple(int(s) for s in np.cumsum(IN_SIZES)[:-1])

kernel_name = "hybrid_chunk_attn_gated_deltanet_adaln"

def rmsnorm(x, g):
    xf = x.astype(jnp.float32)
    y = xf * lax.rsqrt(jnp.mean(xf * xf, axis=-1, keepdims=True) + EPS)
    return (y * g.astype(jnp.float32)).astype(x.dtype)

def l2norm(t):
    return t * lax.rsqrt(jnp.sum(t * t, axis=-1, keepdims=True) + EPS)

def chunk_band_attention(q, k, v, rel_table):
    bsz, seq, h, dh = q.shape
    nc = seq // CHUNK
    band = A_BAND * CHUNK
    qc = q.reshape(bsz, nc, CHUNK, h, dh)
    pad = ((0, 0), (A_PAST_CHUNKS, 0), (0, 0), (0, 0), (0, 0))
    kp = jnp.pad(k.reshape(bsz, nc, CHUNK, h, dh), pad)
    vp = jnp.pad(v.reshape(bsz, nc, CHUNK, h, dh), pad)
    band_idx = jnp.arange(nc)[:, None] + jnp.arange(A_BAND)[None, :]
    kb = kp[:, band_idx].reshape(bsz, nc, band, h, dh)
    vb = vp[:, band_idx].reshape(bsz, nc, band, h, dh)
    s = jnp.einsum('bnqhd,bnkhd->bnhqk', qc, kb).astype(jnp.float32) * (dh ** -0.5)
    qpos = A_PAST_CHUNKS * CHUNK + jnp.arange(CHUNK)
    rel = jnp.clip(qpos[:, None] - jnp.arange(band)[None, :], -A_MAX_REL, A_MAX_REL) + A_MAX_REL
    bias = rel_table.astype(jnp.float32)[:, rel]
    key_chunk = jnp.arange(nc)[:, None] - A_PAST_CHUNKS + (jnp.arange(band) // CHUNK)[None, :]
    valid = (key_chunk >= 0)[None, :, None, None, :]
    s = jnp.where(valid, s + bias[None, None], -1e30)
    p = jax.nn.softmax(s, axis=-1).astype(v.dtype)
    o = jnp.einsum('bnhqk,bnkhd->bnqhd', p, vb)
    return o.reshape(bsz, seq, h * dh)

def causal_depthwise_conv(x, w):
    ch = x.shape[-1]
    return lax.conv_general_dilated(
        x, w[:, None, :], window_strides=(1,), padding=[(CONV_K - 1, 0)],
        dimension_numbers=('NWC', 'WIO', 'NWC'), feature_group_count=ch)

def gated_delta_rule_chunked(q, k, v, g, beta):
    bsz, seq, h, dk = q.shape
    dv = v.shape[-1]
    nc = seq // CHUNK
    to_c = lambda t: t.reshape(bsz, nc, CHUNK, h, t.shape[-1]).transpose(0, 1, 3, 2, 4)
    q, k, v = to_c(q), to_c(k), to_c(v)
    g = g.reshape(bsz, nc, CHUNK, h).transpose(0, 1, 3, 2)
    beta = beta.reshape(bsz, nc, CHUNK, h).transpose(0, 1, 3, 2)
    g_cum = jnp.cumsum(g, axis=-1)
    incl = jnp.tril(jnp.ones((CHUNK, CHUNK), dtype=bool))
    strict = jnp.tril(jnp.ones((CHUNK, CHUNK), dtype=bool), k=-1)
    diff = g_cum[..., :, None] - g_cum[..., None, :]
    decay = jnp.exp(jnp.where(incl, diff, -jnp.inf))
    kk = jnp.einsum('bnhid,bnhjd->bnhij', k, k)
    lower = jnp.where(strict, beta[..., :, None] * kk * decay, 0.0)
    rhs = jnp.concatenate([v * beta[..., None], k * (beta * jnp.exp(g_cum))[..., None]], axis=-1)
    sol = lax.linalg.triangular_solve(lower, rhs, left_side=True, lower=True, unit_diagonal=True)
    u_intra, k_cumdecay = sol[..., :dv], sol[..., dv:]
    qk = jnp.einsum('bnhid,bnhjd->bnhij', q, k) * decay
    q_dec = q * jnp.exp(g_cum)[..., None]
    k_dec = k * jnp.exp(g_cum[..., -1:] - g_cum)[..., None]
    g_last = jnp.exp(g_cum[..., -1])

    def step(state, xs):
        u_i, w_i, qk_i, qd_i, kd_i, gl_i = xs
        u = u_i - jnp.einsum('bhck,bhkv->bhcv', w_i, state)
        o = jnp.einsum('bhck,bhkv->bhcv', qd_i, state) + jnp.einsum('bhij,bhjv->bhiv', qk_i, u)
        state = state * gl_i[..., None, None] + jnp.einsum('bhck,bhcv->bhkv', kd_i, u)
        return state, o

    xs = tuple(jnp.moveaxis(t, 1, 0) for t in (u_intra, k_cumdecay, qk, q_dec, k_dec, g_last))
    s0 = jnp.zeros((bsz, h, dk, dv), jnp.float32)
    _, o = lax.scan(step, s0, xs)
    return o.transpose(1, 0, 3, 2, 4).reshape(bsz, seq, h, dv)

def gated_deltanet(qkv_raw, z, b_raw, a_raw, w_conv, a_log, dt_bias, norm_g):
    bsz, seq, _ = qkv_raw.shape
    qkv = jax.nn.silu(causal_depthwise_conv(qkv_raw, w_conv)).astype(jnp.float32)
    q, k, v = jnp.split(qkv, 3, axis=-1)
    q = l2norm(q.reshape(bsz, seq, B_HEADS, B_HEAD_DIM)) * (B_HEAD_DIM ** -0.5)
    k = l2norm(k.reshape(bsz, seq, B_HEADS, B_HEAD_DIM))
    v = v.reshape(bsz, seq, B_HEADS, B_HEAD_DIM)
    beta = jax.nn.sigmoid(b_raw.astype(jnp.float32))
    g = -jnp.exp(a_log.astype(jnp.float32)) * jax.nn.softplus(
        a_raw.astype(jnp.float32) + dt_bias.astype(jnp.float32))
    o = gated_delta_rule_chunked(q, k, v, g, beta)
    zf = z.astype(jnp.float32).reshape(bsz, seq, B_HEADS, B_HEAD_DIM)
    o = (o * lax.rsqrt(jnp.mean(o * o, axis=-1, keepdims=True) + EPS)
         * norm_g.astype(jnp.float32) * jax.nn.silu(zf))
    return o.reshape(bsz, seq, B_WIDTH).astype(qkv_raw.dtype)

def setup_inputs(seed: int = 0) -> dict:
    key = jax.random.key(seed)
    ks = jax.random.split(key, 18)
    f32 = jnp.float32

    def nrm(k, shape, scale):
        return jax.random.normal(k, shape, f32) * scale

    x = nrm(ks[0], (BATCH, SEQ, D_MODEL), 1.0)
    c = nrm(ks[1], (BATCH, D_MODEL), 1.0)
    w_ada = nrm(ks[2], (DEPTH, D_MODEL, N_MOD * D_MODEL), 0.5 * D_MODEL ** -0.5)
    b_ada = nrm(ks[3], (DEPTH, N_MOD * D_MODEL), 0.02)
    norm1_g = 1.0 + nrm(ks[4], (DEPTH, D_MODEL), 0.02)
    norm2_g = 1.0 + nrm(ks[5], (DEPTH, D_MODEL), 0.02)
    w_in = nrm(ks[6], (DEPTH, D_MODEL, IN_DIM), D_MODEL ** -0.5)
    rel_table = nrm(ks[7], (DEPTH, A_HEADS, 2 * A_MAX_REL + 1), 0.2)
    w_conv = nrm(ks[8], (DEPTH, CONV_K, 3 * B_WIDTH), CONV_K ** -0.5)
    a_log = jnp.log(jax.random.uniform(ks[9], (DEPTH, B_HEADS), f32, 1.0, 16.0))
    dt = jnp.exp(jax.random.uniform(ks[10], (DEPTH, B_HEADS), f32, math.log(1e-3), math.log(1e-1)))
    dt_bias = dt + jnp.log(-jnp.expm1(-dt))
    gdn_norm_g = 1.0 + nrm(ks[11], (DEPTH, B_HEAD_DIM), 0.02)
    w_branch_a = nrm(ks[12], (DEPTH, A_WIDTH, D_MODEL), A_WIDTH ** -0.5)
    w_branch_b = nrm(ks[13], (DEPTH, B_WIDTH, D_MODEL), B_WIDTH ** -0.5)
    w_out = nrm(ks[14], (DEPTH, D_MODEL, D_MODEL), D_MODEL ** -0.5)
    w_ffn_in = nrm(ks[15], (DEPTH, D_MODEL, 2 * FFN_HIDDEN), D_MODEL ** -0.5)
    w_ffn_out = nrm(ks[16], (DEPTH, FFN_HIDDEN, D_MODEL), FFN_HIDDEN ** -0.5)
    final_g = 1.0 + nrm(ks[17], (D_MODEL,), 0.02)
    return {"x": x, "c": c, "w_ada": w_ada, "b_ada": b_ada, "norm1_g": norm1_g,
            "norm2_g": norm2_g, "w_in": w_in, "rel_table": rel_table, "w_conv": w_conv,
            "a_log": a_log, "dt_bias": dt_bias, "gdn_norm_g": gdn_norm_g,
            "w_branch_a": w_branch_a, "w_branch_b": w_branch_b, "w_out": w_out,
            "w_ffn_in": w_ffn_in, "w_ffn_out": w_ffn_out, "final_g": final_g}

def reference(x, c, w_ada, b_ada, norm1_g, norm2_g, w_in, rel_table, w_conv, a_log, dt_bias,
              gdn_norm_g, w_branch_a, w_branch_b, w_out, w_ffn_in, w_ffn_out, final_g):
    bsz, seq, _ = x.shape
    cond = jax.nn.silu(c)
    for l in range(DEPTH):
        mod = (cond @ w_ada[l] + b_ada[l])[:, None, :]
        sh1, sc1, gt1, sh2, sc2, gt2 = jnp.split(mod, N_MOD, axis=-1)
        h = rmsnorm(x, norm1_g[l]) * (1.0 + sc1) + sh1
        proj = h @ w_in[l]
        qa, ka, va, qkvb, zb, bb, ab, ga, gb = jnp.split(proj, IN_SPLITS, axis=-1)
        ya = chunk_band_attention(
            qa.reshape(bsz, seq, A_HEADS, A_HEAD_DIM),
            ka.reshape(bsz, seq, A_HEADS, A_HEAD_DIM),
            va.reshape(bsz, seq, A_HEADS, A_HEAD_DIM), rel_table[l])
        yb = gated_deltanet(qkvb, zb, bb, ab, w_conv[l], a_log[l], dt_bias[l], gdn_norm_g[l])
        merged = (jax.nn.sigmoid(ga) * (ya @ w_branch_a[l])
                  + jax.nn.sigmoid(gb) * (yb @ w_branch_b[l]))
        x = x + gt1 * (merged @ w_out[l])
        h = rmsnorm(x, norm2_g[l]) * (1.0 + sc2) + sh2
        gate, up = jnp.split(h @ w_ffn_in[l], 2, axis=-1)
        x = x + gt2 * ((jax.nn.silu(gate) * up) @ w_ffn_out[l])
    return rmsnorm(x, final_g)


_drawn_inputs = setup_inputs


def setup_inputs(seed=0):
    import zlib

    import numpy as np

    out = dict(_drawn_inputs(seed))
    spreads = {}
    factors = {'b_ada': 3.085,
     'norm1_g': 8.0,
     'norm2_g': 8.0,
     'rel_table': 8.0,
     'a_log': 3.767,
     'gdn_norm_g': 8.0,
     'final_g': 2.881}
    for name, (base, spread) in spreads.items():
        noise = np.random.default_rng([zlib.crc32(name.encode()), seed]).standard_normal(out[name].shape)
        drawn = base * np.exp(spread * noise) if base else spread * noise
        out[name] = jnp.asarray(drawn.astype(out[name].dtype))
    for name, factor in factors.items():
        out[name] = (out[name] * factor).astype(out[name].dtype)
    return out
```

```python
from contextlib import ExitStack

import concourse.bass as bass
from concourse import mybir

F32 = mybir.dt.float32
F32R = mybir.dt.float32r
I32 = mybir.dt.int32
ALU = mybir.AluOpType
ACT = mybir.ActivationFunctionType
AX_X = mybir.AxisListType.X

P = 128
S = 1024
D = 1024
KT = D // P
NT = S // P
HALF = S // 2
EPS = 1e-6
NEG = -1e30
A_H, A_D = 8, 64
A_W = A_H * A_D
B_H, B_D = 4, 128
B_W = B_H * B_D
BAND = 5
SCALE = A_D ** -0.5
EXT = 384
F = 2816
FT = F // P
LEVELS = 7

C_QA, C_KA, C_VA = 0, A_W, 2 * A_W
C_QKVB = 3 * A_W
C_Z = C_QKVB + 3 * B_W
C_AB = C_Z + B_W
C_GA = C_AB + 2 * B_H
C_GB = C_GA + D

V_C, V_ADA, V_N1, V_N2, V_NG = 0, 8, 56, 64, 72
V_ROWS = 73
SH1, SC1, GT1, SH2, SC2, GT2 = (8 * n for n in range(6))

NR = 4
ADA_PER = 8
RSQRT_MAGIC = float(0x5F3759DF)


class Chain:

    def __init__(self, eng, sem, base=0):
        self.eng, self.sem, self.base, self.n = eng, sem, base, 0

    def link(self, ins):
        ins.then_inc(self.sem, 1)
        self.n += 1
        self.eng.wait_ge(self.sem, self.base + self.n)


def bc(ap, n):
    return ap.unsqueeze(2).broadcast_to([ap.shape[0], ap.shape[1], n])


def bc_mid(ap, n):
    return ap.unsqueeze(1).broadcast_to([ap.shape[0], n, ap.shape[1]])


def heads(ap):
    return ap.rearrange("p (h c) -> p h c", h=B_H)


def rsqrt(ch, eng, v, y, t):
    ch.link(eng.tensor_scalar(t.bitcast(I32), v.bitcast(I32), 1, None, ALU.arith_shift_right))
    ch.link(eng.tensor_scalar(y.bitcast(I32), t.bitcast(I32), -1.0, RSQRT_MAGIC, ALU.mult, ALU.add))
    for _ in range(3):
        ch.link(eng.tensor_tensor(t, y, y, ALU.mult))
        ch.link(eng.scalar_tensor_tensor(t, t, -0.5, v, ALU.mult, ALU.mult))
        ch.link(eng.scalar_tensor_tensor(y, t, 1.5, y, ALU.add, ALU.mult))


RSQRT_LINKS = 11


def hybrid_layer(nc, x, c, w_ada, b_ada, norm1_g, norm2_g, w_in, rel_rev, w_conv, a_log, dt_bias,
                 gdn_norm_g, w_branch_a, w_branch_b, w_out, w_ffn_in, w_ffn_out, final_g, out):
    with ExitStack() as ctx:
        def sbin(stack, name, shape, dt=F32):
            return stack.enter_context(nc.sbuf_tensor(name, shape, dt))

        def psin(stack, name, shape):
            return stack.enter_context(nc.psum_tensor(name, shape, F32))

        def sb(name, shape, dt=F32):
            return sbin(ctx, name, shape, dt)

        def sem(name):
            return ctx.enter_context(nc.semaphore(name))

        def dram(name, shape):
            return nc.dram_tensor(name, shape, F32, kind="Internal").ap()

        xT_d = dram("xT_d", [D, S])
        qkvb_d = dram("qkvb_d", [3 * B_W, S])
        qkva_d = dram("qkva_d", [3 * A_W, S])
        z_d = dram("z_d", [B_W, S])
        ga_d = dram("ga_d", [D, S])
        gb_d = dram("gb_d", [D, S])
        ya_d = dram("ya_d", [A_W, S])
        yb_d = dram("yb_d", [B_W, P + S])
        ext_d = dram("ext_d", [A_H, P * EXT])

        act_hi = sb("act_hi", [P, KT, S], F32R)
        act_lo = sb("act_lo", [P, KT, S], F32R)
        w_raw = sb("w_raw", [P, NR, KT, P])
        w_hi = sb("w_hi", [P, 2, KT, P], F32R)
        w_lo = sb("w_lo", [P, 2, KT, P], F32R)
        est = sb("est", [P, 2, S])
        tmp = sb("tmp", [P, S])
        ident = sb("ident", [P, P])
        ones = sb("ones", [P, P])
        incl = sb("incl", [P, P])
        after = sb("after", [P, P])
        lvl = sb("lvl", [P, LEVELS, P])
        vT = sb("vT", [P, V_ROWS])
        wcT = sb("wcT", [P, 48])
        modT = sb("modT", [P, 48])
        gs = sb("gs", [P, KT])
        gs2 = sb("gs2", [P, KT])
        gt1h = sb("gt1h", [P, KT])
        gt2h = sb("gt2h", [P, KT])
        cs = sb("cs", [P, KT])
        cth = sb("cth", [P, KT])
        ss = sb("ss", [P, NT])
        rr = sb("rr", [P, NT])
        rt = sb("rt", [P, NT])
        ngh = sb("ngh", [P, 1])
        negA = sb("negA", [P, B_H])
        dtb = sb("dtb", [P, B_H])
        ab = sb("ab", [P, NT, 2 * B_H])
        ab2 = sb("ab2", [P, NT, 2 * B_H])
        eab = sb("eab", [P, NT, 2 * B_H])
        beta = sb("beta", [P, NT, B_H])
        g = sb("g", [P, NT, B_H])
        u1 = sb("u1", [P, NT, B_H])
        u2 = sb("u2", [P, NT, B_H])
        u3 = sb("u3", [P, NT, B_H])
        eg = sb("eg", [P, 3, NT, B_H])
        neg_egc = sb("neg_egc", [P, NT, B_H])

        with ExitStack() as st0:
            adab = sbin(st0, "adab", [P, 2, KT, 512])
            asum = sbin(st0, "asum", [P, 2 * D])
            xr = sbin(st0, "xr", [P, 2, D])
            xT0 = sbin(st0, "xT0", [P, KT, S])
            vrow = sbin(st0, "vrow", [V_ROWS, P])
            wcrow = sbin(st0, "wcrow", [48, P])
            rrow = sbin(st0, "rrow", [A_H, 257])
            ext = sbin(st0, "ext", [A_H, EXT])
        dg0 = tmp[:, :].rearrange("p (t q) -> p t q", t=NT)
        with ExitStack() as st1:
            def b1(n):
                return sbin(st1, n, [P, B_H * P])
            gst = sbin(st1, "gst", [P, 12, P])
            kd, vn, Ec, Lt, At, gm = (b1(n) for n in ("kd", "vn", "Ec", "Lt", "At", "gm"))
            Tm, Um, Ym, Xm, ym, St, om, on, ybst, junk = (b1(n) for n in (
                "Tm", "Um", "Ym", "Xm", "ym", "St", "om", "on", "ybst", "junk"))
            Ct = sbin(st1, "Ct", [P, 3, B_H * P])
            sskq = sbin(st1, "sskq", [P, 8])
            vkq = sbin(st1, "vkq", [P, 8])
            rkq = sbin(st1, "rkq", [P, 8])
            tkq = sbin(st1, "tkq", [P, 8])
            cj = sbin(st1, "cj", [P, 4])
            cr = sbin(st1, "cr", [P, 4])
            nk = sbin(st1, "nk", [P, 4])
            rq = sbin(st1, "rq", [P, 4])
            sso = sbin(st1, "sso", [P, 4])
            vo = sbin(st1, "vo", [P, 4])
            ro = sbin(st1, "ro", [P, 4])
            to = sbin(st1, "to", [P, 4])
            a_raw = sbin(st1, "a_raw", [P, 2, KT, P])
            asc = sbin(st1, "asc", [P, 2, P])
            ast = sbin(st1, "ast", [P, 3, S])
            bias = sbin(st1, "bias", [P, 2, 2 * P])
            Pm = sbin(st1, "Pm", [P, BAND * P])
            PT = sbin(st1, "PT", [P, BAND * P])
            V = sbin(st1, "V", [P, 2, NT, A_D])
            yast = sbin(st1, "yast", [P, S])
            mx = sbin(st1, "mx", [P, 2])
            negm = sbin(st1, "negm", [P, 2])
            psm = sbin(st1, "psm", [P, 2])
            rsm = sbin(st1, "rsm", [P, 2])
        with ExitStack() as st2:
            yst = sbin(st2, "yst", [P, 2, S])
            zst = sbin(st2, "zst", [P, S])
            gst2 = sbin(st2, "gst2", [P, 2, S])
            y_hi = sbin(st2, "y_hi", [P, 8, S], F32R)
            y_lo = sbin(st2, "y_lo", [P, 8, S], F32R)
        with ExitStack() as st3:
            xT = sbin(st3, "xT", [P, KT, S])
            f_raw = sbin(st3, "f_raw", [P, 2, S])
            o_hi = sbin(st3, "o_hi", [P, 2, S], F32R)
            o_lo = sbin(st3, "o_lo", [P, 2, S], F32R)
            h_hi = sbin(st3, "h_hi", [P, 2, 2, S], F32R)
            h_lo = sbin(st3, "h_lo", [P, 2, 2, S], F32R)
        with ExitStack() as st4:
            sbin(st4, "xT_kept", [P, KT, S])
            frow = sbin(st4, "frow", [P, NT, D])
            gbc = sbin(st4, "gbc", [P, D])
        with ExitStack() as pst:
            ps = [psin(pst, f"ps{n}", [P, S]) for n in range(2)]
            aS = psin(pst, "aS", [P, S])
            aT = psin(pst, "aT", [P, HALF])
            gps = psin(pst, "gps", [P, HALF])
        with ExitStack() as pst2:
            pm = [psin(pst2, f"pm{n}", [P, S]) for n in range(4)]

        vec_in, rel_in, misc_in = sem("vec_in"), sem("rel_in"), sem("misc_in")
        ada_in = [sem("ada_in0"), sem("ada_in1")]
        xr_in = [sem("xr_in0"), sem("xr_in1")]
        consts_ready, ext_ready, ext_stored = sem("consts_ready"), sem("ext_ready"), sem("ext_stored")
        pool_chain, vec_chain, act_chain = sem("pool_chain"), sem("vec_chain"), sem("act_chain")
        vecT_mm, vecT_ready = sem("vecT_mm"), sem("vecT_ready")
        xt_mm, xt_read, xT_stored = sem("xt_mm"), sem("xt_read"), sem("xT_stored")
        ss_ready, diag_ready, rb_mm = sem("ss_ready"), sem("diag_ready"), sem("rb_mm")
        asum_ready, mod_mm, mod_ready = sem("asum_ready"), sem("mod_mm"), sem("mod_ready")
        xn_ready, hi_ready, lo_ready = sem("xn_ready"), sem("hi_ready"), sem("lo_ready")
        raw_in = [sem(f"raw_in{n}") for n in range(NR)]
        wa_in = sem("wa_in")
        whi_ready, wlo_ready, dense_mm = sem("whi_ready"), sem("wlo_ready"), sem("dense_mm")
        est_ready = sem("est_ready")
        est_stored = [sem("est_stored0"), sem("est_stored1")]
        tap_ready, taps_ready, th_ready = sem("tap_ready"), sem("taps_ready"), sem("th_ready")
        ab_read, abT_mm, ab_abs, ab_exp, g_ready, gc_mm, eg_ready = (sem(n) for n in (
            "ab_read", "abT_mm", "ab_abs", "ab_exp", "g_ready", "gc_mm", "eg_ready"))
        gst_in, gst_free, gdn_mm, gdn_read = sem("gst_in"), sem("gst_free"), sem("gdn_mm"), sem("gdn_read")
        gm_ready, ssk_ready, ssq_ready, cj_ready, cr_ready, nk_ready = (sem(n) for n in (
            "gm_ready", "ssk_ready", "ssq_ready", "cj_ready", "cr_ready", "nk_ready"))
        ec_ready, ct_ready, u0_ready, vn_ready, kd_ready, neg_ready, S_zero = (sem(n) for n in (
            "ec_ready", "ct_ready", "u0_ready", "vn_ready", "kd_ready", "neg_ready", "S_zero"))
        sso_ready, on_ready, yb_stored = sem("sso_ready"), sem("on_ready"), sem("yb_stored")
        a_in = [sem("a_in0"), sem("a_in1")]
        asc_ready, adam_mm, ada_all = sem("asc_ready"), sem("adam_mm"), sem("ada_all")
        ast_in = [sem("ast_in0"), sem("ast_in1")]
        ast_free = [sem("ast_free0"), sem("ast_free1")]
        bias_in, bias_masked, bias_free = sem("bias_in"), sem("bias_masked"), sem("bias_free")
        sc_mm, negm_ready, exp_ready, pn_ready = (sem(n) for n in ("sc_mm", "negm_ready", "exp_ready", "pn_ready"))
        at_mm, at_read, pv_mm, pv_read, ya_stored = (sem(n) for n in (
            "at_mm", "at_read", "pv_mm", "pv_read", "ya_stored"))
        y_in = [sem("y_in0"), sem("y_in1")]
        z_in, yz_ready, yhi_ready, ylo_ready = sem("z_in"), sem("yz_ready"), sem("yhi_ready"), sem("ylo_ready")
        gate_in, merged_ready, pair_free = sem("gate_in"), sem("merged_ready"), sem("pair_free")
        mhi_ready, mlo_ready = sem("mhi_ready"), sem("mlo_ready")
        xT_in, x2_ready, sq_ready, sqs_ready = sem("xT_in"), sem("x2_ready"), sem("sq_ready"), sem("sqs_ready")
        ss2_mm, diag2_ready, rb2_mm = sem("ss2_mm"), sem("diag2_ready"), sem("rb2_mm")
        o_in = [sem("o_in0"), sem("o_in1")]
        ohi_ready, olo_ready, o_mm, po_free = sem("ohi_ready"), sem("olo_ready"), sem("o_mm"), sem("po_free")
        gth_ready, gu_read, hhi_ready, hlo_ready = sem("gth_ready"), sem("gu_read"), sem("hhi_ready"), sem("hlo_ready")
        gbc_in, ft_mm, ft_read, fss_ready, fr_ready = (sem(n) for n in (
            "gbc_in", "ft_mm", "ft_read", "fss_ready", "fr_ready"))
        row_ready, out_stored = sem("row_ready"), sem("out_stored")

        D_CONV, D_A, D_B, D_M, D_O, D_F = 5, 13, 29, 45, 53, 61

        def raw_count(ds, i=0):
            return 16 * (ds // NR + 1) + 16 * i

        w_ada_v = w_ada.rearrange("(k p) c -> p k c", p=P)
        w_in_v = w_in.rearrange("(k p) c -> p k c", p=P)
        w_a_v = w_branch_a.rearrange("(k p) c -> p k c", p=P)
        w_b_v = w_branch_b.rearrange("(k p) c -> p k c", p=P)
        w_o_v = w_out.rearrange("(k p) c -> p k c", p=P)
        w_f_v = w_ffn_in.rearrange("(k p) c -> p k c", p=P)

        (Q_TO, Q_TK, Q_TQ, Q_TV, Q_D, Q_QS, Q_GK, Q_GQ, Q_KS, Q_T0) = range(10)
        Q_L1 = 10
        Q_Y, Q_AY, Q_KY = 27, 28, 29
        NQ = 30
        GSLOT = [1, 2, 3, 4, 5, 6, 7, 8, 9] + list(range(10, 31))
        Q_AT = {s: q for q, s in enumerate(GSLOT)}
        SC_AT = [0, 1, 3, 5, 7, 9, 11, 13, 15, 16, 17, 19, 21, 23, 25, 27, 29]
        VT_AT = [0, 14]

        def level_of(q):
            s, part = divmod(q - Q_L1, 3)
            if s == 5 and part == 1:
                part = 2
            return s + 1, part

        def at_index(m=None, e=None):
            if m is None:
                return 8 * e
            return m + 1 if m <= 6 else m + 2

        def fifth(s):
            return ps[(D_B + s // 8 + 1) % 2][:, 0:P]

        def hd(t, h):
            return t[:, h * P:(h + 1) * P]

        def ext_skew(h):
            v = ext_d[bass.ds(h, 1), P - 1:P - 1 + P * (EXT - 1)]
            return v.rearrange("a (p n) -> (a p) n", n=EXT - 1)[:, 0:2 * P]

        block = ctx.enter_context(nc.Block())

        @block.sync
        def _(sp):
            def load_unit(ds, i, view, col):
                if ds >= NR:
                    sp.wait_ge(wlo_ready, ds - NR + 1 + 4 * i)
                sp.dma_start(w_raw[:, ds % NR], view[:, :, bass.ds(col, P)]).then_inc(raw_in[ds % NR], 16)

            for row, v in ((V_C, c), (V_ADA, b_ada), (V_N1, norm1_g), (V_N2, norm2_g), (V_NG, gdn_norm_g)):
                n = v.shape[0] // P
                sp.dma_start(vrow[row:row + n, :], v.rearrange("(r q) -> r q", q=P)).then_inc(vec_in, 16)
            sp.dma_start(wcrow[:, :], w_conv.rearrange("t (g q) -> (t g) q", q=P)).then_inc(vec_in, 16)
            for n in range(4):
                if n >= 2:
                    sp.wait_ge(asum_ready, n - 1)
                sp.dma_start(adab[:, n % 2], w_ada_v[:, :, n * 512:(n + 1) * 512]).then_inc(ada_in[n % 2], 16)
                for t in (2 * n, 2 * n + 1):
                    if t >= 2:
                        sp.wait_ge(ss_ready, t - 1)
                        sp.wait_ge(xt_mm, t - 1)
                    sp.dma_start(xr[:, t % 2, :], x[t * P:(t + 1) * P, :]).then_inc(xr_in[t % 2], 16)
            sp.dma_start(rrow[:, :], rel_rev).then_inc(rel_in, 16)
            sp.dma_start(negA[:, :], bass.AP(a_log.tensor, 0, [[0, P], [1, B_H]])).then_inc(misc_in, 16)
            sp.dma_start(dtb[:, :], bass.AP(dt_bias.tensor, 0, [[0, P], [1, B_H]])).then_inc(misc_in, 16)
            for d in range(D_A):
                load_unit(d, 0, w_in_v, C_AB if d == 0 else C_QKVB + (d - 1) * P)
                if d == 5:
                    sp.wait_ge(xt_read, NT)
                    sp.dma_start(xT_d.rearrange("(k p) t -> p k t", p=P), xT0[:, :, :]).then_inc(xT_stored, 16)
                    sp.wait_ge(ext_ready, 1)
                    sp.dma_start(ext_d.rearrange("h (p n) -> h p n", n=EXT),
                                 ext[:, :].unsqueeze(1).broadcast_to([A_H, P, EXT])).then_inc(ext_stored, 16)

            def load_gst(t):
                sp.wait_ge(gst_free, t)
                sp.dma_start(gst[:, :, :], qkvb_d.rearrange("(g q) t -> q g t", q=P)[:, :, bass.ds(t * P, P)])\
                    .then_inc(gst_in, 16)

            with sp.Fori(0, 4) as i:
                for j, col in enumerate((C_QA, C_KA, C_VA, C_Z)):
                    load_unit(D_A + j, i, w_in_v, i * P + col)
                    if j == 0:
                        sp.wait_ge(xT_stored, 16)
                        sp.wait_ge(lo_ready, KT)
                    if j == 1:
                        sp.wait_ge(est_stored[0], 16 * 6)
                        sp.wait_ge(est_stored[1], 16 * 6)
                        load_gst(i)
                    for a in (2 * j, 2 * j + 1):
                        sp.wait_ge(asc_ready, i * ADA_PER + max(a - 1, 0))
                        sp.dma_start(a_raw[:, a % 2], w_ada_v[:, :, bass.ds(i * (ADA_PER * P) + (2 * D + a * P), P)])\
                            .then_inc(a_in[a % 2], 16)

            def load_heads(i, e):
                sp.wait_ge(ast_free[e], i)
                for n, base in enumerate((C_QA, C_KA, C_VA)):
                    sp.dma_start(ast[e * A_D:(e + 1) * A_D, n, :], qkva_d[bass.ds(i * P + (base + e * A_D), A_D), :])\
                        .then_inc(ast_in[e], 16)

            with sp.Fori(0, 4) as i:
                for j, col in enumerate((C_GA, C_GA + P, C_GB, C_GB + P)):
                    load_unit(D_B + j, i, w_in_v, i * (2 * P) + col)
                load_gst(i + 4)
                sp.wait_ge(est_stored[0], 16 * 14)
                sp.wait_ge(est_stored[1], 16 * 14)
                load_heads(i, 0)
                sp.wait_ge(ext_stored, 16)
                sp.wait_ge(bias_free, i)
                for e in range(2):
                    sp.dma_start(bias[:, e, :], ext_skew(i * 2 + e)).then_inc(bias_in, 16)
                load_heads(i, 1)

            def load_merge_unit(ds, i):
                sp.wait_ge(wlo_ready, ds - NR + 1 + 4 * i)
                cols = bass.ds(i * (4 * P) + (ds - D_M) * P, P)
                sp.dma_start(w_raw[:, ds % NR, 0:4], w_a_v[:, :, cols]).then_inc(wa_in, 16)
                sp.wait_ge(wa_in, 16 * (ds - D_M + 1))
                sp.dma_start(w_raw[:, ds % NR, 4:8], w_b_v[:, :, cols]).then_inc(raw_in[ds % NR], 16)

            for j in range(4):
                load_merge_unit(D_M + j, 0)
            sp.wait_ge(ya_stored, 64)
            sp.wait_ge(yb_stored, 16 * 9)
            for k in range(8):
                if k >= 2:
                    sp.wait_ge(ylo_ready, k - 1)
                src = ya_d[k * P:(k + 1) * P, :] if k < 4 else yb_d[(k - 4) * P:(k - 3) * P, P:P + S]
                sp.dma_start(yst[:, k % 2, :], src).then_inc(y_in[k % 2], 16)
                if k >= 4:
                    if k >= 5:
                        sp.wait_ge(yz_ready, k - 4)
                    sp.dma_start(zst[:, :], z_d[(k - 4) * P:(k - 3) * P, :]).then_inc(z_in, 16)
            sp.wait_ge(est_stored[0], 16 * 22)
            sp.wait_ge(est_stored[1], 16 * 22)

            def load_gates(b):
                sp.wait_ge(pair_free, b + 2)
                for n, t in enumerate((ga_d, gb_d)):
                    sp.dma_start(gst2[:, n, :], t[bass.ds(b * P, P), :]).then_inc(gate_in, 16)

            for b in range(4):
                load_gates(b)
                load_merge_unit(D_M + 4 + b, 0)
            for b in range(4, 8):
                load_gates(b)
                load_unit(D_O + b - 4, 0, w_o_v, (b - 4) * P)
            sp.wait_ge(dense_mm, D_O)
            sp.wait_ge(pair_free, 10)
            sp.dma_start(xT[:, :, :], xT_d.rearrange("(k p) t -> p k t", p=P)).then_inc(xT_in, 16)
            for b in range(4, 8):
                load_unit(D_O + b, 0, w_o_v, b * P)

            def load_pair(ds, i, col):
                load_unit(ds, i, w_f_v, col)
                load_unit(ds + 1, i, w_f_v, col + F)

            def load_o(n, i):
                for e in range(2):
                    if n >= 2:
                        sp.wait_ge(olo_ready, n - 1 + e + 4 * i)
                    sp.dma_start(f_raw[:, e, :], w_ffn_out[bass.ds(i * (4 * P) + (n + e) * P, P), :])\
                        .then_inc(o_in[e], 16)

            load_pair(D_F, 0, 0)
            load_pair(D_F + 2, 0, P)
            load_o(0, 0)
            with sp.Fori(0, 4) as it:
                for u in range(2):
                    ds = D_F + 4 * (1 + u)
                    load_pair(ds, it * 2, it * (4 * P) + (2 + 2 * u) * P)
                    load_pair(ds + 2, it * 2, it * (4 * P) + (3 + 2 * u) * P)
                    load_o(2 * (1 + u), it)
            for n in (9, 10):
                load_pair(D_F + 4 * n, 0, 2 * n * P)
                load_pair(D_F + 4 * n + 2, 0, (2 * n + 1) * P)
                load_o(2 * n, 0)
            sp.wait_ge(o_mm, 8 * 11)
            sp.dma_start(gbc[:, :], bass.AP(final_g.tensor, 0, [[0, P], [1, D]])).then_inc(gbc_in, 16)
            for t in range(NT):
                sp.wait_ge(row_ready, t + 1)
                sp.dma_start(out[t * P:(t + 1) * P, :], frow[:, t, :]).then_inc(out_stored, 16)
            sp.wait_ge(out_stored, 16 * NT)

        @block.gpsimd
        def _(pool):
            ch = Chain(pool, pool_chain)
            pool.memset(ident[:, :], 0.0).then_inc(pool_chain, 1)
            pool.memset(ones[:, :], 1.0).then_inc(pool_chain, 1)
            pool.memset(incl[:, :], 1.0).then_inc(pool_chain, 1)
            pool.memset(after[:, :], 1.0).then_inc(pool_chain, 1)
            pool.memset(lvl[:, :, :], 0.0).then_inc(pool_chain, 1)
            pool.memset(ext[:, :], 0.0).then_inc(pool_chain, 1)
            ch.n = 6
            pool.wait_ge(pool_chain, 6)
            pool.affine_select(out=ident[:, :], in_=ident[:, :], compare_op=ALU.not_equal, fill=1.0,
                               base=0, pattern=[[-1, P]], channel_multiplier=1).then_inc(consts_ready, 1)
            pool.affine_select(out=incl[:, :], in_=incl[:, :], compare_op=ALU.is_ge, fill=0.0,
                               base=0, pattern=[[1, P]], channel_multiplier=-1).then_inc(consts_ready, 1)
            pool.affine_select(out=after[:, :], in_=after[:, :], compare_op=ALU.is_ge, fill=0.0,
                               base=-1, pattern=[[-1, P]], channel_multiplier=1).then_inc(consts_ready, 1)
            for s in range(LEVELS):
                b = 1 << s
                odd = lvl[:, s, :].rearrange("p (n two b) -> p n two b", two=2, b=b)[:, :, 1, :]
                nb = P // (2 * b)
                ch.link(pool.memset(odd, 1.0))
                ch.link(pool.affine_select(out=odd, in_=odd, compare_op=ALU.is_ge, fill=0.0, base=0,
                                           pattern=[[-2 * b, nb], [0, b]], channel_multiplier=1))
                ch.link(pool.affine_select(out=odd, in_=odd, compare_op=ALU.is_ge, fill=0.0, base=b - 1,
                                           pattern=[[2 * b, nb], [0, b]], channel_multiplier=-1))
            pool.wait_ge(rel_in, 16)
            pool.tensor_scalar(ext[:, P - 1:EXT], rrow[:, :], rrow[:, 0:1], 1.0 / SCALE,
                               ALU.subtract, ALU.mult).then_inc(ext_ready, 1)

            def wait_apart(s, value):
                value = pool.to_reg(value)
                pool.wait_ge(ext_ready, 1)
                pool.wait_ge(s, value)

            def store(ds, i, dst):
                if ds < D_CONV:
                    pool.wait_ge(est_ready, ds)
                else:
                    wait_apart(est_ready, ds + 4 * i)
                pool.dma_start(dst, est[:, ds % 2, :]).then_inc(est_stored[ds % 2], 16)

            for d in range(1, D_CONV):
                store(d, 0, qkvb_d[(d - 1) * P:d * P, :])
            with pool.Fori(0, 2) as i:
                for j in range(4):
                    store(D_CONV + j, i, qkvb_d[bass.ds(i * (4 * P) + (D_CONV + j - 1) * P, P), :])
            pool.wait_ge(lo_ready, KT)
            pool.wait_ge(xT_stored, 16)
            pool.memset(St[:, :], 0.0).then_inc(S_zero, 1)
            pool.memset(on[:, :], 0.0).then_inc(on_ready, 1)

            def gdn_slot(t, s):
                if s == 0:
                    pool.wait_ge(eg_ready, 1)
                    pool.wait_ge(gdn_mm, t * NQ)
                    pool.tensor_tensor(heads(gm[:, :]), bc_mid(incl[:, :], B_H), bc(g_of(t), P), ALU.mult)\
                        .then_inc(gm_ready, 1)
                q = Q_AT.get(s)
                if q == Q_TO:
                    wait_apart(gdn_read, t * NQ + Q_TO + 1)
                    pool.dma_start(yb_d.rearrange("(h q) t -> q h t", q=P)[:, :, bass.ds(t * P, P)],
                                   heads(ybst[:, :])).then_inc(yb_stored, 16)
                if q == Q_QS:
                    pool.wait_ge(gdn_read, t * NQ + Q_D + 1)
                    ch.link(pool.tensor_tensor(heads(Ec[:, :]), heads(Ec[:, :]), bc_mid(incl[:, :], B_H), ALU.mult))
                    pool.wait_ge(cj_ready, t + 1)
                    pool.tensor_tensor(heads(Ec[:, :]), heads(Ec[:, :]), bc(cj[:, :], P), ALU.mult)\
                        .then_inc(ec_ready, 1)
                if q == Q_GQ:
                    pool.wait_ge(gdn_read, t * NQ + Q_GK + 1)
                    for s_ in range(3):
                        pool.tensor_tensor(heads(Ct[:, s_, :]), heads(Lt[:, :]), bc_mid(lvl[:, s_, :], B_H),
                                           ALU.mult).then_inc(ct_ready, 1)
                    pool.wait_ge(nk_ready, t + 1)
                    pool.wait_ge(gdn_read, t * NQ + Q_TV + 1)
                    pool.tensor_tensor(heads(vn[:, :]), heads(vn[:, :]), bc(nk[:, :], P), ALU.mult)\
                        .then_inc(vn_ready, 1)
                if q == Q_L1:
                    pool.wait_ge(cr_ready, t + 1)
                    pool.wait_ge(ssk_ready, t * B_H + B_H)
                    pool.tensor_tensor(heads(kd[:, :]), heads(kd[:, :]), bc(cr[:, :], P), ALU.mult)\
                        .then_inc(kd_ready, 1)
                    pool.wait_ge(u0_ready, t + 1)
                    pool.tensor_tensor(heads(Ct[:, 0, :]), heads(Lt[:, :]), bc_mid(lvl[:, 3, :], B_H),
                                       ALU.mult).then_inc(ct_ready, 1)
                for lv in (4, 5, 6):
                    if q == Q_L1 + 3 * (lv - 4) + 1:
                        pool.wait_ge(gdn_mm, t * NQ + Q_L1 + 3 * (lv - 4) + 1)
                        pool.tensor_tensor(heads(Ct[:, lv % 3, :]), heads(Lt[:, :]), bc_mid(lvl[:, lv, :], B_H),
                                           ALU.mult).then_inc(ct_ready, 1)

            def g_of(t):
                return g[:, bass.ds(t, 1), :].rearrange("p a h -> p (a h)")

            pool_base = ch.n
            with pool.Fori(0, 4) as i:
                ch = Chain(pool, pool_chain, i + pool_base)
                for s in range(32):
                    gdn_slot(i, s)
                    if s in (13, 21, 29):
                        j = s // 8 - 1
                        store(D_A + j, i, qkva_d[bass.ds(i * P + j * A_W, P), :])
                store(D_A + 3, i, z_d[bass.ds(i * P, P), :])
                assert ch.n == 1
            pool_base += 4
            with pool.Fori(0, 4) as i:
                ch = Chain(pool, pool_chain, i + pool_base)
                for s in range(32):
                    gdn_slot(i + 4, s)
                    if s in (13, 21, 29):
                        j = s // 8 - 1
                        store(D_B + j, i, (ga_d, ga_d, gb_d)[j][bass.ds(i * (2 * P) + (0, P, 0)[j], P), :])
                store(D_B + 3, i, gb_d[bass.ds(i * (2 * P) + P, P), :])
                wait_apart(pv_read, i * 16 + 16)
                pool.dma_start(ya_d[bass.ds(i * P, P), :], yast[:, :]).then_inc(ya_stored, 16)
            pool.wait_ge(gdn_read, NT * NQ + 1)
            pool.dma_start(yb_d.rearrange("(h q) t -> q h t", q=P)[:, :, S:S + P], heads(ybst[:, :]))\
                .then_inc(yb_stored, 16)
            for b in range(1, 8):
                pool.wait_ge(sq_ready, b + 1)
                if b > 1:
                    pool.wait_ge(sqs_ready, b - 1)
                pool.tensor_tensor(tmp[:, :], tmp[:, :], est[:, b % 2, :], ALU.add).then_inc(sqs_ready, 1)

        @block.tensor
        def _(pe):
            def dense_k(ds, k, dst, hi, lo, first, last):
                for n, (wt, at) in enumerate(((w_hi, hi), (w_hi, lo), (w_lo, hi))):
                    for h in range(2):
                        cols = slice(h * HALF, (h + 1) * HALF)
                        ins = pe.matmul(dst[:, cols], wt[:, ds % 2, k, :], at[:, cols],
                                        start=(first and n == 0), stop=(last and n == 2))
                return ins

            def unit_k(ds, i, k, dst):
                if k == 0:
                    pe.wait_ge(wlo_ready, ds + 1 + 4 * i)
                    if ds >= 3:
                        pe.wait_ge(est_ready, ds - 2 + 4 * i)
                    elif ds == 2:
                        pe.wait_ge(ab_read, 1)
                ins = dense_k(ds, k, dst, act_hi[:, k, :], act_lo[:, k, :], k == 0, k == KT - 1)
                if k == KT - 1:
                    ins.then_inc(dense_mm, 1)

            pe.wait_ge(consts_ready, 3)
            pe.wait_ge(vec_in, 16 * 6)
            pe.transpose(gps[:, 0:V_ROWS], vrow[:, :], ident[0:V_ROWS, 0:V_ROWS])
            pe.transpose(gps[:, 128:176], wcrow[:, :], ident[0:48, 0:48]).then_inc(vecT_mm, 1)
            for t in range(NT):
                pe.wait_ge(xr_in[t % 2], 16 * (t // 2 + 1))
                if t >= 2:
                    pe.wait_ge(xt_read, t - 1)
                for k in range(KT):
                    ins = pe.transpose(ps[t % 2][:, k * P:(k + 1) * P], xr[:, t % 2, k * P:(k + 1) * P],
                                       ident[:, :])
                ins.then_inc(xt_mm, 1)
            pe.wait_ge(diag_ready, 1)
            for t in range(NT):
                ins = pe.matmul(aS[:, t * P:(t + 1) * P], ones[:, :], dg0[:, t, :], start=True, stop=True)
            ins.then_inc(rb_mm, 1)
            pe.wait_ge(vecT_ready, 2)
            for q in range(16):
                if q % 4 == 0:
                    pe.wait_ge(asum_ready, q // 4 + 1)
                ins = pe.matmul(gps[:, q:q + 1], asum[:, q * P:(q + 1) * P], ones[:, 0:1], start=True, stop=True)
            ins.then_inc(mod_mm, 1)
            pe.wait_ge(xt_read, NT)
            for d in range(D_CONV):
                for k in range(KT):
                    if d == 0:
                        pe.wait_ge(lo_ready, k + 1)
                    unit_k(d, 0, k, ps[d % 2])
                if d == 1:
                    pe.wait_ge(ab_read, 1)
                    pe.wait_ge(mod_ready, 1)
                    for t in range(NT):
                        ins = pe.transpose(gps[:, t * 8:(t + 1) * 8], est[0:8, 0, t * P:(t + 1) * P],
                                           ident[0:8, 0:8])
                    ins.then_inc(abT_mm, 1)
                if d == 3:
                    pe.wait_ge(g_ready, 1)
                    for n, m in enumerate((incl, after, ones)):
                        ins = pe.matmul(gps[:, n * 32:(n + 1) * 32], m[:, :],
                                        g[:, :, :].rearrange("p t h -> p (t h)"), start=True, stop=True)
                    ins.then_inc(gc_mm, 1)
            with pe.Fori(0, 2) as i:
                for j in range(4):
                    for k in range(KT):
                        unit_k(D_CONV + j, i, k, ps[(D_CONV + j) % 2])
            pe.wait_ge(eg_ready, 1)
            pe.wait_ge(S_zero, 1)

            def gdn_step(t, q):
                pe.wait_ge(gdn_read, t * NQ + q)
                if q == Q_TO:
                    pe.wait_ge(on_ready, t + 1)
                    for h in range(B_H):
                        ins = pe.transpose(hd(gps, h), hd(on, h), ident[:, :])
                elif q in (Q_TK, Q_TQ, Q_TV):
                    if q == Q_TK:
                        pe.wait_ge(gst_in, t * 16 + 16)
                    base = {Q_TQ: 0, Q_TK: 4, Q_TV: 8}[q]
                    for h in range(B_H):
                        ins = pe.transpose(hd(gps, h), gst[:, base + h, :], ident[:, :])
                elif q == Q_D:
                    pe.wait_ge(gm_ready, t + 1)
                    ins = pe.matmul(gps[:, :], after[:, :], gm[:, :], start=True, stop=True)
                elif q in (Q_QS, Q_KS):
                    for h in range(B_H):
                        ins = pe.matmul(hd(gps, h), gst[:, (0 if q == Q_QS else 4) + h, :], hd(St, h),
                                        start=True, stop=True)
                elif q in (Q_GK, Q_GQ):
                    for h in range(B_H):
                        ins = pe.matmul(hd(gps, h), gst[:, 4 + h, :], gst[:, (4 if q == Q_GK else 0) + h, :],
                                        start=True, stop=True)
                elif q == Q_T0:
                    pe.wait_ge(u0_ready, t + 1)
                    for h in range(B_H):
                        ins = pe.transpose(hd(gps, h), hd(Um, h), ident[:, :])
                        if h == 0:
                            ins.then_inc(gst_free, 1)
                elif q == Q_Y:
                    for h in range(B_H):
                        ins = pe.matmul(hd(gps, h), hd(Um, h), hd(Xm, h), start=True, stop=True)
                elif q == Q_AY:
                    for h in range(B_H):
                        ins = pe.matmul(hd(gps, h), hd(At, h), hd(ym, h), start=True, stop=True)
                elif q == Q_KY:
                    pe.wait_ge(kd_ready, t + 1)
                    for h in range(B_H):
                        ins = pe.matmul(hd(gps, h), hd(kd, h), hd(ym, h), start=True, stop=True)
                else:
                    lv, part = level_of(q)
                    for h in range(B_H):
                        if part == 0:
                            if h == 0:
                                pe.wait_ge(ct_ready, t * LEVELS + lv + 1)
                            ins = pe.matmul(hd(gps, h), Ct[:, lv % 3, h * P:(h + 1) * P], hd(Tm, h),
                                            start=True, stop=True)
                        elif part == 1:
                            ins = pe.matmul(hd(gps, h), hd(Um, h), hd(Ym, h), start=True, stop=True)
                        elif lv < LEVELS - 1:
                            ins = pe.transpose(hd(gps, h), hd(Tm, h), ident[:, :])
                        else:
                            ins = pe.matmul(hd(gps, h), hd(Ym, h), hd(Um, h), start=True, stop=True)
                ins.then_inc(gdn_mm, 1)

            with pe.Fori(0, 4) as i:
                for s in range(32):
                    if s in Q_AT:
                        gdn_step(i, Q_AT[s])
                    unit_k(D_A + s // 8, i, s % 8, ps[(D_A + s // 8) % 2])
                    if s % 4 == 3:
                        a = s // 4
                        pe.wait_ge(asc_ready, i * ADA_PER + a + 1)
                        pe.matmul(aS[:, bass.ds(i * ADA_PER + a, 1)], asc[:, a % 2, :], ones[:, 0:1],
                                  start=True, stop=True).then_inc(adam_mm, 1)
            pe.wait_ge(ada_all, 1)

            def attention_slot(i, s):
                for m in range(16):
                    e, qt = divmod(m, NT)
                    nk_ = min(BAND, qt + 1)
                    rows = slice(e * A_D, (e + 1) * A_D)
                    if s == SC_AT[m + 1] + 1:
                        pe.wait_ge(at_read, i * 18 + at_index(m=m) + 1)
                        for kt in range(nk_):
                            ins = pe.matmul(aT[0:A_D, 0:P], V[:, e, qt - nk_ + 1 + kt, :],
                                            PT[:, kt * P:(kt + 1) * P], start=(kt == 0), stop=(kt == nk_ - 1))
                        ins.then_inc(pv_mm, 1)
                    if s == SC_AT[m + 1]:
                        pe.wait_ge(pn_ready, i * 16 + m + 1)
                        pe.wait_ge(at_read, i * 18 + at_index(m=m))
                        pe.wait_ge(pv_read, i * 16 + m)
                        if nk_ == BAND:
                            pe.wait_ge(est_ready, D_B + s // 8 - 1 + 4 * i)
                        for kt in range(nk_):
                            dst = aT[:, kt * P:(kt + 1) * P] if kt < 4 else fifth(s)
                            ins = pe.transpose(dst, Pm[:, kt * P:(kt + 1) * P], ident[:, :])
                            if kt == 0 and m % 8 == 7:
                                ins.then_inc(ast_free[e], 1)
                        ins.then_inc(at_mm, 1)
                    if s == SC_AT[m]:
                        pe.wait_ge(exp_ready, i * 16 + m)
                        if m % NT == 0:
                            pe.wait_ge(ast_in[e], i * 48 + 48)
                        k0 = (qt - nk_ + 1) * P
                        w = nk_ * P
                        ins = pe.matmul(aS[:, 0:min(w, 512)], ast[rows, 0, qt * P:(qt + 1) * P],
                                        ast[rows, 1, k0:k0 + min(w, 512)], start=True, stop=True)
                        if w > 512:
                            ins = pe.matmul(aS[:, 512:w], ast[rows, 0, qt * P:(qt + 1) * P],
                                            ast[rows, 1, k0 + 512:k0 + w], start=True, stop=True)
                        ins.then_inc(sc_mm, 1)
                for e in range(2):
                    if s == VT_AT[e]:
                        landed = pe.to_reg(i * 48 + 48)
                        copied = pe.to_reg(i * 18 + at_index(e=e))
                        yT_read = pe.to_reg(i * 16 + 7 * e)
                        pe.wait_ge(ada_all, 1)
                        pe.wait_ge(ast_in[e], landed)
                        pe.wait_ge(at_read, copied)
                        pe.wait_ge(pv_read, yT_read)
                        rows = slice(e * A_D, (e + 1) * A_D)
                        for kt in range(NT):
                            ins = pe.transpose(aT[:, kt * A_D:(kt + 1) * A_D], ast[rows, 2, kt * P:(kt + 1) * P],
                                               ident[rows, rows])
                        ins.then_inc(at_mm, 1)

            with pe.Fori(0, 4) as i:
                for s in range(32):
                    attention_slot(i, s)
                    if s in Q_AT:
                        gdn_step(i + 4, Q_AT[s])
                    unit_k(D_B + s // 8, i, s % 8, ps[(D_B + s // 8) % 2])
            gdn_step(NT, Q_TO)

            pe.wait_ge(pair_free, 2)
            for b in range(8):
                d = D_M + b
                pe.wait_ge(wlo_ready, d + 1)
                pe.wait_ge(pair_free, b + 1)
                for k in range(8):
                    if b == 0:
                        pe.wait_ge(ylo_ready, k + 1)
                    ins = dense_k(d, k, pm[2 * (b % 2) + k // 4], y_hi[:, k, :], y_lo[:, k, :],
                                  k % 4 == 0, k % 4 == 3)
                ins.then_inc(dense_mm, 1)
            for b in range(8):
                d = D_O + b
                pe.wait_ge(wlo_ready, d + 1)
                if b == 0:
                    pe.wait_ge(pair_free, 9)
                if b >= 4:
                    pe.wait_ge(x2_ready, b - 3)
                for k in range(8):
                    if b == 0:
                        pe.wait_ge(mlo_ready, k + 1)
                    ins = dense_k(d, k, pm[b % 4], act_hi[:, k, :], act_lo[:, k, :], k == 0, k == 7)
                ins.then_inc(dense_mm, 1)
            pe.wait_ge(sqs_ready, 7)
            pe.wait_ge(x2_ready, 8)
            for t in range(NT):
                ins = pe.matmul(pm[0][:, t:t + 1], tmp[:, t * P:(t + 1) * P], ones[:, 0:1], start=True, stop=True)
            ins.then_inc(ss2_mm, 1)
            pe.wait_ge(diag2_ready, 1)
            for t in range(NT):
                ins = pe.matmul(pm[1][:, t * P:(t + 1) * P], ones[:, :], dg0[:, t, :], start=True, stop=True)
            ins.then_inc(rb2_mm, 1)

            def gate_up(n, i, first=False):
                for e in range(2):
                    ds = D_F + 2 * n + e
                    pe.wait_ge(wlo_ready, ds + 1 + 8 * i)
                    if e == 0:
                        pe.wait_ge(gu_read, n + 4 * i)
                    for k in range(KT):
                        if first and e == 0:
                            pe.wait_ge(lo_ready, KT + k + 1)
                        ins = dense_k(ds, k, pm[e], act_hi[:, k, :], act_lo[:, k, :], k == 0, k == 7)
                    ins.then_inc(dense_mm, 1)

            def ffn_out(p, i, bs):
                for b in bs:
                    if b == 0:
                        pe.wait_ge(hlo_ready, 2 * p + 2 + 4 * i)
                        pe.wait_ge(olo_ready, 2 * p + 2 + 4 * i)
                    pe.wait_ge(po_free, 8 * p + b + 1 + 16 * i)
                    dst = pm[2 + b % 2]
                    for e in range(2):
                        for n, (wt, at) in enumerate(((o_hi, h_hi), (o_hi, h_lo), (o_lo, h_hi))):
                            for h in range(2):
                                cols = slice(h * HALF, (h + 1) * HALF)
                                ins = pe.matmul(dst[:, cols], wt[:, e, b * P:(b + 1) * P], at[:, p % 2, e, cols],
                                                start=(e == 0 and n == 0), stop=(e == 1 and n == 2))
                    ins.then_inc(o_mm, 1)

            def ffn_body(n, i):
                gate_up(2 * n, i)
                ffn_out(n - 1, i, range(4))
                gate_up(2 * n + 1, i)
                ffn_out(n - 1, i, range(4, 8))

            gate_up(0, 0, first=True)
            gate_up(1, 0)
            with pe.Fori(0, 4) as it:
                ffn_body(1, it)
                ffn_body(2, it)
            ffn_body(9, 0)
            ffn_body(10, 0)
            ffn_out(10, 0, range(8))
            for b in range(8):
                pe.wait_ge(po_free, 8 * 10 + b + 3)
                if b == 0:
                    pe.wait_ge(gu_read, FT)
                if b >= 2:
                    pe.wait_ge(ft_read, b - 1)
                for t in range(NT):
                    ins = pe.transpose(pm[b % 2][:, t * P:(t + 1) * P], xT[:, b, t * P:(t + 1) * P], ident[:, :])
                ins.then_inc(ft_mm, 1)

        @block.scalar
        def _(act):
            def split_hi(ds, i=0):
                act.wait_ge(raw_in[ds % NR], raw_count(ds, i))
                if ds >= 2:
                    act.wait_ge(dense_mm, ds - 1 + 4 * i)
                act.activation(w_hi[:, ds % 2], w_raw[:, ds % NR], ACT.Copy).then_inc(whi_ready, 1)

            act.wait_ge(vecT_mm, 1)
            act.activation(vT[:, :], gps[:, 0:V_ROWS], ACT.Copy).then_inc(vecT_ready, 1)
            act.wait_ge(vecT_ready, 1)
            act.activation(cth[:, :], vT[:, V_C:V_C + 8], ACT.Tanh, scale=0.5).then_inc(act_chain, 1)
            act.activation(wcT[:, :], gps[:, 128:176], ACT.Copy, scale=0.5).then_inc(vecT_ready, 1)
            act.activation(ngh[:, :], vT[:, V_NG:V_NG + 1], ACT.Copy, scale=0.5).then_inc(act_chain, 1)
            for t in range(NT):
                act.wait_ge(xr_in[t % 2], 16 * (t // 2 + 1))
                if t:
                    act.wait_ge(ss_ready, t)
                act.activation(tmp[:, :], xr[:, t % 2, :], ACT.Square, accum_out=ss[:, t:t + 1])\
                    .then_inc(ss_ready, 1)
                act.wait_ge(xt_mm, t + 1)
                act.activation(xT0[:, :, t * P:(t + 1) * P], ps[t % 2][:, :].rearrange("p (k q) -> p k q", k=KT),
                               ACT.Copy).then_inc(xt_read, 1)
            act.wait_ge(misc_in, 32)
            act.activation(negA[:, :], negA[:, :], ACT.Exp).then_inc(act_chain, 1)
            split_hi(0)
            split_hi(1)
            for k in range(KT):
                act.wait_ge(xn_ready, k + 1)
                act.activation(act_hi[:, k, :], est[:, k % 2, :], ACT.Identity,
                               bias=modT[:, SH1 + k:SH1 + k + 1]).then_inc(hi_ready, 1)

            def evac_conv(ds, i, d, col):
                act.wait_ge(dense_mm, ds + 1 + 4 * i)
                act.wait_ge(est_ready, ds - 1 + 4 * i)
                if ds >= 3:
                    act.wait_ge(est_stored[ds % 2], 16 * ((ds - 1) // 2) + 32 * i)
                act.activation(est[:, ds % 2, :], ps[ds % 2][:, :], ACT.Copy, scale=col).then_inc(tap_ready, 1)
                split_hi(ds + 2, i)
                act.wait_ge(taps_ready, ds + 4 * i)
                act.activation(tmp[:, :], est[:, ds % 2, :], ACT.Tanh).then_inc(th_ready, 1)

            for d in range(D_CONV):
                if d == 0:
                    act.wait_ge(dense_mm, 1)
                    act.wait_ge(lo_ready, KT)
                    act.activation(est[0:8, 0, :], ps[0][0:8, :], ACT.Copy).then_inc(ab_read, 1)
                    split_hi(2)
                    continue
                if d == 2:
                    act.wait_ge(abT_mm, 1)
                evac_conv(d, 0, d, wcT[:, 36 + d - 1:36 + d])
                if d == 2:
                    act.wait_ge(ab_abs, 1)
                    act.activation(eab[:, :, :], eab[:, :, :], ACT.Exp, scale=-1.0).then_inc(ab_exp, 1)
                if d == 4:
                    act.wait_ge(gc_mm, 1)
                    act.activation(eg[:, :, :, :].rearrange("p a t h -> p (a t h)"), gps[:, 0:96], ACT.Exp)\
                        .then_inc(eg_ready, 1)
            with act.Fori(0, 2) as i:
                for j in range(4):
                    evac_conv(D_CONV + j, i, None, wcT[:, bass.ds(i * 4 + (36 + D_CONV + j - 1), 1)])

            def gdn_read_act(t, q):
                lv = part = None
                if Q_L1 <= q < Q_Y:
                    lv, part = level_of(q)
                copies = {Q_TV: vn, Q_T0: Tm, Q_Y: ym}
                dst = copies.get(q)
                if part == 0:
                    dst = Ym
                if part == 2 and lv < LEVELS - 1:
                    dst = Um
                if dst is not None:
                    act.wait_ge(gdn_mm, t * NQ + q + 1)
                    act.activation(dst[:, :], gps[:, :], ACT.Copy).then_inc(gdn_read, 1)
                if q == Q_TO:
                    act.wait_ge(gdn_mm, t * NQ + q + 1)
                    act.wait_ge(yb_stored, t * 16)
                    act.activation(ybst[:, :], gps[:, :], ACT.Copy, scale=ngh[:, :]).then_inc(gdn_read, 1)
                if q == Q_TQ:
                    act.wait_ge(gdn_mm, t * NQ + q + 1)
                    for h in range(B_H):
                        ins = act.activation(hd(junk, h), hd(gps, h), ACT.Square, accum_out=sskq[:, 4 + h:5 + h])
                    ins.then_inc(gdn_read, 1)
                    act.wait_ge(gdn_read, t * NQ + q + 1)
                    for h in range(B_H):
                        act.activation(hd(junk, h), hd(kd, h), ACT.Square, accum_out=sskq[:, h:h + 1])\
                            .then_inc(ssk_ready, 1)
                if q == Q_D:
                    act.wait_ge(gdn_mm, t * NQ + q + 1)
                    act.activation(Ec[:, :], gps[:, :], ACT.Exp).then_inc(gdn_read, 1)
                if q == Q_KY:
                    act.wait_ge(gdn_read, t * NQ + Q_AY + 1)
                    for h in range(B_H):
                        act.activation(hd(junk, h), hd(om, h), ACT.Square, accum_out=sso[:, h:h + 1])\
                            .then_inc(sso_ready, 1)

            def evac(ds, i, kind):
                act.wait_ge(dense_mm, ds + 1 + 4 * i)
                act.wait_ge(est_ready, ds - 1 + 4 * i)
                if kind == "z":
                    act.activation(tmp[:, :], ps[ds % 2][:, :], ACT.Tanh, scale=0.5).then_inc(th_ready, 1)
                else:
                    act.wait_ge(est_stored[ds % 2], 16 * ((ds - 1) // 2) + 32 * i)
                    if kind == "copy":
                        act.activation(est[:, ds % 2, :], ps[ds % 2][:, :], ACT.Copy).then_inc(est_ready, 1)
                    else:
                        act.activation(est[:, ds % 2, :], ps[ds % 2][:, :], ACT.Tanh, scale=0.5)\
                            .then_inc(est_ready, 1)
                split_hi(ds + 2, i)

            with act.Fori(0, 4) as i:
                for s in range(32):
                    if s % 8 == 0 and s:
                        evac(D_A + s // 8 - 1, i, "copy")
                    if s in Q_AT:
                        gdn_read_act(i, Q_AT[s])
                evac(D_A + 3, i, "z")

            def attention_act(i, s):
                for m in range(16):
                    e, qt = divmod(m, NT)
                    w = min(BAND, qt + 1) * P
                    if s == SC_AT[m + 1] + 1:
                        act.wait_ge(pv_mm, i * 16 + m + 1)
                        if m == 0:
                            act.wait_ge(ya_stored, i * 16)
                        act.activation(yast[e * A_D:(e + 1) * A_D, qt * P:(qt + 1) * P], aT[0:A_D, 0:P],
                                       ACT.Copy).then_inc(pv_read, 1)
                    if s == SC_AT[m + 1]:
                        act.wait_ge(at_mm, i * 18 + at_index(m=m) + 1)
                        ins = act.activation(PT[:, 0:min(w, 512)], aT[:, 0:min(w, 512)], ACT.Copy)
                        if w > 512:
                            ins = act.activation(PT[:, 512:w], fifth(s), ACT.Copy)
                        ins.then_inc(at_read, 1)
                for e in range(2):
                    if s == VT_AT[e]:
                        act.wait_ge(at_mm, i * 18 + at_index(e=e) + 1)
                        act.activation(V[:, e].rearrange("p a b -> p (a b)"), aT[:, :], ACT.Copy)\
                            .then_inc(at_read, 1)

            def exp_act(i, s):
                for m in range(16):
                    if s == SC_AT[m]:
                        w = min(BAND, m % NT + 1) * P
                        act.wait_ge(negm_ready, i * 16 + m + 1)
                        act.activation(Pm[:, 0:w], aS[:, 0:w], ACT.Exp, scale=SCALE, bias=negm[:, m % 2:m % 2 + 1],
                                       accum_out=psm[:, m % 2:m % 2 + 1]).then_inc(exp_ready, 1)

            with act.Fori(0, 4) as i:
                for s in range(32):
                    attention_act(i, s)
                    if s in Q_AT:
                        gdn_read_act(i + 4, Q_AT[s])
                    exp_act(i, s)
                    if s % 8 == 0 and s:
                        evac(D_B + s // 8 - 1, i, "tanh")
                evac(D_B + 3, i, "tanh")
            gdn_read_act(NT, Q_TO)
            for k in range(8):
                act.wait_ge(y_in[k % 2], 16 * (k // 2 + 1))
                if k >= 4:
                    act.wait_ge(yz_ready, k - 3)
                act.activation(y_hi[:, k, :], yst[:, k % 2, :], ACT.Copy).then_inc(yhi_ready, 1)
            for b in range(8):
                split_hi(D_M + b + 2)
                act.wait_ge(merged_ready, b + 1)
                act.activation(act_hi[:, b, :], est[:, b % 2, :], ACT.Copy).then_inc(mhi_ready, 1)
            for b in range(8):
                split_hi(D_O + b + 2)
                act.wait_ge(x2_ready, b + 1)
                dst = tmp[:, :] if b == 0 else est[:, b % 2, :]
                if b >= 3:
                    act.wait_ge(sqs_ready, b - 2)
                if b == 0:
                    act.wait_ge(merged_ready, 8)
                if b in (1, 2):
                    act.wait_ge(mlo_ready, 8)
                act.activation(dst, xT[:, b, :], ACT.Square).then_inc(sq_ready, 1)
            for k in range(KT):
                act.wait_ge(xn_ready, KT + k + 1)
                act.activation(act_hi[:, k, :], est[:, k % 2, :], ACT.Identity,
                               bias=modT[:, SH2 + k:SH2 + k + 1]).then_inc(hi_ready, 1)

            def ffn_hidden(n, i, ahead=True):
                ds = D_F + 2 * n
                act.wait_ge(dense_mm, ds + 1 + 8 * i)
                if ahead:
                    split_hi(ds + 2, 2 * i)
                act.wait_ge(gu_read, n + 4 * i)
                act.activation(est[:, 0, :], pm[0][:, :], ACT.Tanh, scale=0.5).then_inc(gth_ready, 1)
                if ahead:
                    split_hi(ds + 3, 2 * i)
                act.wait_ge(gu_read, n + 1 + 4 * i)
                act.activation(h_hi[:, (n // 2) % 2, n % 2, :], est[:, 1, :], ACT.Copy).then_inc(hhi_ready, 1)

            def split_o(p, i):
                for e in range(2):
                    act.wait_ge(o_in[e], 16 * (p + 1) + 32 * i)
                    act.wait_ge(o_mm, 8 * p + 16 * i)
                    act.activation(o_hi[:, e, :], f_raw[:, e, :], ACT.Copy).then_inc(ohi_ready, 1)

            ffn_hidden(0, 0)
            ffn_hidden(1, 0)
            with act.Fori(0, 4) as it:
                for n in (1, 2):
                    split_o(n - 1, it)
                    ffn_hidden(2 * n, it)
                    ffn_hidden(2 * n + 1, it)
            for n in (9, 10):
                split_o(n - 1, 0)
                ffn_hidden(2 * n, 0)
                ffn_hidden(2 * n + 1, 0, ahead=(n < 10))
            split_o(10, 0)
            for b in range(8):
                act.wait_ge(ft_mm, b + 1)
                act.activation(frow[:, :, b * P:(b + 1) * P], pm[b % 2][:, :].rearrange("p (t q) -> p t q", t=NT),
                               ACT.Copy).then_inc(ft_read, 1)
            act.wait_ge(ft_read, 8)
            for t in range(NT):
                if t:
                    act.wait_ge(fss_ready, t)
                act.activation(tmp[:, :], frow[:, t, :], ACT.Square, accum_out=ss[:, t:t + 1]).then_inc(fss_ready, 1)

        @block.vector
        def _(dve):
            ch = Chain(dve, vec_chain)

            def split_lo(ds, i=0):
                dve.wait_ge(whi_ready, ds + 1 + 4 * i)
                dve.tensor_tensor(w_lo[:, ds % 2], w_raw[:, ds % NR], w_hi[:, ds % 2].bitcast(F32), ALU.subtract)\
                    .then_inc(wlo_ready, 1)

            dve.wait_ge(act_chain, 1)
            ch.link(dve.scalar_tensor_tensor(cs[:, :], cth[:, :], 1.0, vT[:, V_C:V_C + 8], ALU.add, ALU.mult))
            ch.link(dve.tensor_scalar(cs[:, :], cs[:, :], 0.5, None, ALU.mult))
            for n in range(4):
                dve.wait_ge(ada_in[n % 2], 16 * (n // 2 + 1))
                dst = asum[:, n * 512:(n + 1) * 512]
                ch.link(dve.tensor_scalar(dst, adab[:, n % 2, 0, :], cs[:, 0:1], None, ALU.mult))
                for k in range(1, KT):
                    ins = dve.scalar_tensor_tensor(dst, adab[:, n % 2, k, :], cs[:, k:k + 1], dst,
                                                   ALU.mult, ALU.add)
                    if k < KT - 1:
                        ch.link(ins)
                ins.then_inc(asum_ready, 1)
            dve.wait_ge(ss_ready, NT)
            ch.link(dve.tensor_scalar(ss[:, :], ss[:, :], 1.0 / D, EPS, ALU.mult, ALU.add))
            rsqrt(ch, dve, ss[:, :], rr[:, :], rt[:, :])
            dve.wait_ge(consts_ready, 3)
            dve.tensor_tensor(dg0, bc_mid(ident[:, :], NT), bc(rr[:, :], P), ALU.mult).then_inc(diag_ready, 1)
            dve.wait_ge(mod_mm, 1)
            dve.tensor_tensor(modT[:, 0:16], gps[:, 0:16], vT[:, V_ADA:V_ADA + 16], ALU.add).then_inc(mod_ready, 1)
            dve.wait_ge(mod_ready, 1)
            ch.link(dve.scalar_tensor_tensor(gs[:, :], modT[:, SC1:SC1 + 8], 1.0, vT[:, V_N1:V_N1 + 8],
                                             ALU.add, ALU.mult))
            dve.wait_ge(rb_mm, 1)
            dve.wait_ge(xt_read, NT)
            split_lo(0)

            def norm_tile(k, x_t, gain, rb, sh, n0):
                if k >= 2:
                    dve.wait_ge(lo_ready, n0 + k - 1)
                dve.scalar_tensor_tensor(est[:, k % 2, :], x_t, gain, rb, ALU.mult, ALU.mult).then_inc(xn_ready, 1)
                dve.wait_ge(hi_ready, n0 + k + 1)
                dve.scalar_tensor_tensor(act_lo[:, k, :], est[:, k % 2, :], modT[:, sh + k:sh + k + 1],
                                         act_hi[:, k, :].bitcast(F32), ALU.add, ALU.subtract).then_inc(lo_ready, 1)

            for k in range(KT):
                norm_tile(k, xT0[:, k, :], gs[:, k:k + 1], aS[:, :], SH1, 0)
            split_lo(1)

            def conv(ds, i, taps):
                split_lo(ds + 2, i)
                dve.wait_ge(tap_ready, ds + 4 * i)
                e, q = est[:, ds % 2, :], ps[ds % 2]
                for s, w in zip((1, 2, 3), taps):
                    ins = dve.scalar_tensor_tensor(e[:, s:], q[:, 0:S - s], w, e[:, s:], ALU.mult, ALU.add)
                    if s < 3:
                        ch.link(ins)
                ins.then_inc(taps_ready, 1)
                dve.wait_ge(th_ready, ds + 4 * i)
                dve.scalar_tensor_tensor(e, tmp[:, :], 1.0, e, ALU.add, ALU.mult).then_inc(est_ready, 1)

            for d in range(D_CONV):
                if d == 0:
                    split_lo(2)
                    continue
                conv(d, 0, [wcT[:, (3 - s) * 12 + d - 1:(3 - s) * 12 + d] for s in (1, 2, 3)])
                if d == 1:
                    dve.wait_ge(abT_mm, 1)
                    dve.wait_ge(misc_in, 32)
                    ch.link(dve.tensor_copy(ab[:, :, :], gps[:, 0:64].rearrange("p (t h) -> p t h", t=NT)))
                    ch.link(dve.tensor_tensor(ab[:, :, 4:8], ab[:, :, 4:8], bc_mid(dtb[:, :], NT), ALU.add))
                    ch.link(dve.tensor_scalar(ab2[:, :, :], ab[:, :, :], -1.0, None, ALU.mult))
                    dve.tensor_tensor(eab[:, :, :], ab[:, :, :], ab2[:, :, :], ALU.max).then_inc(ab_abs, 1)
                if d == 2:
                    dve.wait_ge(ab_exp, 1)
                    eb, ea = eab[:, :, 0:4], eab[:, :, 4:8]
                    ch.link(dve.tensor_scalar(u1[:, :, :], ab[:, :, 0:4], 0.0, None, ALU.is_ge))
                    ch.link(dve.tensor_scalar(u2[:, :, :], eb, -1.0, 1.0, ALU.mult, ALU.add))
                    ch.link(dve.tensor_tensor(u1[:, :, :], u1[:, :, :], u2[:, :, :], ALU.mult))
                    ch.link(dve.tensor_tensor(u1[:, :, :], u1[:, :, :], eb, ALU.add))
                    ch.link(dve.tensor_scalar(u2[:, :, :], eb, 1.0, None, ALU.add))
                    ch.link(dve.reciprocal(u2[:, :, :], u2[:, :, :]))
                    ch.link(dve.tensor_tensor(beta[:, :, :], u1[:, :, :], u2[:, :, :], ALU.mult))
                    ch.link(dve.tensor_scalar(u1[:, :, :], ea, 2.0, None, ALU.add))
                    ch.link(dve.reciprocal(u1[:, :, :], u1[:, :, :]))
                    ch.link(dve.tensor_tensor(u1[:, :, :], u1[:, :, :], ea, ALU.mult))
                    ch.link(dve.tensor_tensor(u2[:, :, :], u1[:, :, :], u1[:, :, :], ALU.mult))
                    ch.link(dve.tensor_scalar(u3[:, :, :], u2[:, :, :], 1.0 / 15, None, ALU.mult))
                    for n in (13, 11, 9, 7, 5, 3):
                        ch.link(dve.scalar_tensor_tensor(u3[:, :, :], u3[:, :, :], 1.0 / n, u2[:, :, :],
                                                         ALU.add, ALU.mult))
                    ch.link(dve.scalar_tensor_tensor(u3[:, :, :], u3[:, :, :], 1.0, u1[:, :, :],
                                                     ALU.add, ALU.mult))
                    ch.link(dve.tensor_scalar(u2[:, :, :], ab[:, :, 4:8], 0.0, None, ALU.max))
                    ch.link(dve.scalar_tensor_tensor(u3[:, :, :], u3[:, :, :], 2.0, u2[:, :, :],
                                                     ALU.mult, ALU.add))
                    dve.wait_ge(act_chain, 3)
                    ch.link(dve.tensor_tensor(u3[:, :, :], u3[:, :, :], bc_mid(negA[:, :], NT), ALU.mult))
                    dve.tensor_scalar(g[:, :, :], u3[:, :, :], -1.0, None, ALU.mult).then_inc(g_ready, 1)
            base = ch.n
            with dve.Fori(0, 2) as i:
                ch = Chain(dve, vec_chain, i * 8 + base)
                for j in range(4):
                    ds = D_CONV + j
                    conv(ds, i, [wcT[:, bass.ds(i * 4 + (3 - s) * 12 + ds - 1, 1)] for s in (1, 2, 3)])
                assert ch.n == 8
            base += 16
            dve.wait_ge(eg_ready, 1)
            dve.tensor_scalar(neg_egc[:, :, :], eg[:, 0], -1.0, None, ALU.mult).then_inc(neg_ready, 1)
            dve.wait_ge(neg_ready, 1)

            def by_head(t3, t):
                return t3[:, bass.ds(t, 1), :].rearrange("p a h -> p (a h)")

            def gdn_dve(t, q):
                done = t * NQ + q + 1
                lv = part = None
                if Q_L1 <= q < Q_Y:
                    lv, part = level_of(q)
                if q == Q_TK:
                    dve.wait_ge(gdn_mm, done)
                    dve.tensor_copy(kd[:, :], gps[:, :]).then_inc(gdn_read, 1)
                if q == Q_TV:
                    dve.wait_ge(ssk_ready, t * 4 + 4)
                    ch.link(dve.tensor_scalar(vkq[:, :], sskq[:, :], EPS, None, ALU.add))
                    ch.link(dve.reciprocal(cr[:, :], vkq[:, 0:4]))
                    dve.tensor_tensor(cj[:, :], cr[:, :], by_head(beta, t), ALU.mult).then_inc(cj_ready, 1)
                    dve.wait_ge(cj_ready, t + 1)
                    dve.tensor_tensor(cr[:, :], cj[:, :], by_head(eg[:, 1], t), ALU.mult).then_inc(cr_ready, 1)
                    rsqrt(ch, dve, vkq[:, :], rkq[:, :], tkq[:, :])
                    ch.link(dve.tensor_scalar(rq[:, :], rkq[:, 4:8], B_D ** -0.5, None, ALU.mult))
                    dve.tensor_tensor(nk[:, :], vkq[:, 0:4], rkq[:, 0:4], ALU.mult).then_inc(nk_ready, 1)
                if q == Q_QS:
                    dve.wait_ge(gdn_mm, done)
                    dve.tensor_tensor(heads(om[:, :]), heads(gps[:, :]), bc(by_head(eg[:, 0], t), P), ALU.mult)\
                        .then_inc(gdn_read, 1)
                if q in (Q_GK, Q_GQ):
                    dve.wait_ge(gdn_mm, done)
                    dve.wait_ge(ec_ready, t + 1)
                    dve.tensor_tensor((Lt if q == Q_GK else At)[:, :], gps[:, :], Ec[:, :], ALU.mult)\
                        .then_inc(gdn_read, 1)
                if q == Q_KS:
                    dve.wait_ge(gdn_mm, done)
                    dve.wait_ge(vn_ready, t + 1)
                    for h in range(B_H):
                        ins = dve.scalar_tensor_tensor(hd(Xm, h), hd(gps, h), by_head(neg_egc, t)[:, h:h + 1],
                                                       hd(vn, h), ALU.mult, ALU.add)
                    ins.then_inc(gdn_read, 1)
                    dve.wait_ge(ct_ready, t * LEVELS + 1)
                    dve.tensor_tensor(heads(Um[:, :]), bc_mid(ident[:, :], B_H), heads(Ct[:, 0, :]),
                                      ALU.subtract).then_inc(u0_ready, 1)
                if part == 1:
                    dve.wait_ge(gdn_mm, done)
                    dve.tensor_tensor(Tm[:, :], Tm[:, :], gps[:, :], ALU.subtract).then_inc(gdn_read, 1)
                if part == 2 and lv == LEVELS - 1:
                    dve.wait_ge(gdn_mm, done)
                    dve.tensor_tensor(Um[:, :], Um[:, :], gps[:, :], ALU.subtract).then_inc(gdn_read, 1)
                if q == Q_AY:
                    dve.wait_ge(gdn_mm, done)
                    dve.tensor_tensor(om[:, :], om[:, :], gps[:, :], ALU.add).then_inc(gdn_read, 1)
                if q == Q_KY:
                    dve.wait_ge(gdn_mm, done)
                    for h in range(B_H):
                        ins = dve.scalar_tensor_tensor(hd(St, h), hd(St, h), by_head(eg[:, 2], t)[:, h:h + 1],
                                                       hd(gps, h), ALU.mult, ALU.add)
                    ins.then_inc(gdn_read, 1)

            def gdn_out(t):
                dve.wait_ge(sso_ready, t * 4 + 4)
                ch.link(dve.tensor_tensor(vo[:, :], sso[:, :], rq[:, :], ALU.mult))
                ch.link(dve.tensor_tensor(vo[:, :], vo[:, :], rq[:, :], ALU.mult))
                ch.link(dve.tensor_scalar(vo[:, :], vo[:, :], 1.0 / B_D, EPS, ALU.mult, ALU.add))
                rsqrt(ch, dve, vo[:, :], ro[:, :], to[:, :])
                ch.link(dve.tensor_tensor(ro[:, :], ro[:, :], rq[:, :], ALU.mult))
                dve.tensor_tensor(heads(on[:, :]), heads(om[:, :]), bc(ro[:, :], P), ALU.mult).then_inc(on_ready, 1)

            def ada_unit(i, a):
                dve.wait_ge(a_in[a % 2], i * (16 * ADA_PER // 2) + 16 * (a // 2 + 1))
                ch.link(dve.tensor_tensor(a_raw[:, a % 2], a_raw[:, a % 2], bc(cs[:, :], P), ALU.mult))
                dve.wait_ge(adam_mm, i * ADA_PER + max(a - 1, 0))
                dve.tensor_reduce(asc[:, a % 2, :], a_raw[:, a % 2].rearrange("p k c -> p c k"), AX_X, ALU.add)\
                    .then_inc(asc_ready, 1)

            LINKS_GDN = 2 + RSQRT_LINKS + 1 + 4 + RSQRT_LINKS
            LINKS_A = LINKS_GDN + ADA_PER
            with dve.Fori(0, 4) as i:
                ch = Chain(dve, vec_chain, i * LINKS_A + base)
                for s in range(32):
                    if s in Q_AT:
                        gdn_dve(i, Q_AT[s])
                    if s % 8 == 0 and s:
                        split_lo(D_A + s // 8 + 1, i)
                    if s % 4 == 1:
                        ada_unit(i, s // 4)
                gdn_out(i)
                dve.wait_ge(th_ready, i + 13)
                dve.wait_ge(est_stored[(D_A + 3) % 2], 16 * ((D_A + 2) // 2) + 32 * i)
                dve.scalar_tensor_tensor(est[:, (D_A + 3) % 2, :], tmp[:, :], 1.0, ps[(D_A + 3) % 2][:, :],
                                         ALU.add, ALU.mult).then_inc(est_ready, 1)
                split_lo(D_A + 5, i)
                assert ch.n == LINKS_A, ch.n
            base += 4 * LINKS_A
            ch = Chain(dve, vec_chain, base)
            dve.wait_ge(adam_mm, 4 * ADA_PER)
            dve.tensor_tensor(modT[:, 16:48], aS[:, 0:32], vT[:, V_ADA + 16:V_ADA + 48], ALU.add).then_inc(ada_all, 1)
            dve.wait_ge(ada_all, 1)
            ch.link(dve.scalar_tensor_tensor(gs2[:, :], modT[:, SC2:SC2 + 8], 1.0, vT[:, V_N2:V_N2 + 8],
                                             ALU.add, ALU.mult))
            ch.link(dve.tensor_scalar(gt1h[:, :], modT[:, GT1:GT1 + 8], 0.5, None, ALU.mult))
            ch.link(dve.tensor_scalar(gt2h[:, :], modT[:, GT2:GT2 + 8], 0.5, None, ALU.mult))
            base += ch.n

            def scores_dve(i, m):
                e, qt = divmod(m, NT)
                w = min(BAND, qt + 1) * P
                dve.wait_ge(sc_mm, i * 16 + m + 1)
                near = aS[:, max(w - 2 * P, 0):w]
                ins = dve.tensor_tensor(near, near, bias[:, e, 2 * P - min(w, 2 * P):2 * P], ALU.add)
                if m == 15:
                    ins.then_inc(bias_free, 1)
                    dve.wait_ge(bias_free, i + 1)
                else:
                    ch.link(ins)
                if w == BAND * P:
                    ch.link(dve.memset(aS[A_D:P, 0:A_D], NEG))
                ch.link(dve.tensor_reduce(mx[:, m % 2:m % 2 + 1], aS[:, 0:w], AX_X, ALU.max))
                dve.tensor_scalar(negm[:, m % 2:m % 2 + 1], mx[:, m % 2:m % 2 + 1], -SCALE, None, ALU.mult)\
                    .then_inc(negm_ready, 1)

            def normalise(i, m):
                w = min(BAND, m % NT + 1) * P
                dve.wait_ge(exp_ready, i * 16 + m + 1)
                ch.link(dve.reciprocal(rsm[:, m % 2:m % 2 + 1], psm[:, m % 2:m % 2 + 1]))
                dve.tensor_scalar(Pm[:, 0:w], Pm[:, 0:w], rsm[:, m % 2:m % 2 + 1], None, ALU.mult)\
                    .then_inc(pn_ready, 1)

            LINKS_B = LINKS_GDN + 1 + 16 + 8 + 16 + 15
            with dve.Fori(0, 4) as i:
                ch = Chain(dve, vec_chain, i * LINKS_B + base)
                dve.wait_ge(bias_in, i * 32 + 32)
                ch.link(dve.memset(bias[0:A_D, :, 3 * A_D:4 * A_D], NEG))
                for s in range(32):
                    for m in range(16):
                        if SC_AT[m] == s - 1 and SC_AT[m + 1] == s:
                            normalise(i, m)
                    for m in range(16):
                        if SC_AT[m] == s:
                            scores_dve(i, m)
                    if s in Q_AT:
                        gdn_dve(i + 4, Q_AT[s])
                    if s % 8 == 0 and s:
                        split_lo(D_B + s // 8 + 1, i)
                    for m in range(16):
                        if SC_AT[m] == s - 1 and SC_AT[m + 1] == s + 1:
                            normalise(i, m)
                gdn_out(i + 4)
                split_lo(D_B + 5, i)
                assert ch.n == LINKS_B, (ch.n, LINKS_B)
            base += 4 * LINKS_B
            ch = Chain(dve, vec_chain, base)
            dve.wait_ge(est_stored[0], 16 * 22)
            dve.wait_ge(est_stored[1], 16 * 22)
            dve.wait_ge(pv_read, 64)
            dve.wait_ge(gdn_read, NT * NQ + 1)
            dve.memset(vo[:, 0:1], 0.0).then_inc(pair_free, 1)
            dve.memset(vo[:, 1:2], 0.0).then_inc(pair_free, 1)
            for k in range(8):
                dve.wait_ge(y_in[k % 2], 16 * (k // 2 + 1))
                if k >= 4:
                    dve.wait_ge(z_in, 16 * (k - 3))
                    dve.tensor_tensor(yst[:, k % 2, :], yst[:, k % 2, :], zst[:, :], ALU.mult).then_inc(yz_ready, 1)
                dve.wait_ge(yhi_ready, k + 1)
                dve.tensor_tensor(y_lo[:, k, :], yst[:, k % 2, :], y_hi[:, k, :].bitcast(F32), ALU.subtract)\
                    .then_inc(ylo_ready, 1)
            for b in range(8):
                split_lo(D_M + b + 2)
                e = est[:, b % 2, :]
                dve.wait_ge(gate_in, 32 * (b + 1))
                dve.wait_ge(dense_mm, D_M + b + 1)
                ch.link(dve.scalar_tensor_tensor(e, gst2[:, 0, :], 1.0, pm[2 * (b % 2)][:, :], ALU.add, ALU.mult))
                dve.scalar_tensor_tensor(tmp[:, :], gst2[:, 1, :], 1.0, pm[2 * (b % 2) + 1][:, :],
                                         ALU.add, ALU.mult).then_inc(pair_free, 1)
                dve.wait_ge(pair_free, b + 3)
                dve.tensor_tensor(e, e, tmp[:, :], ALU.add).then_inc(merged_ready, 1)
                dve.wait_ge(mhi_ready, b + 1)
                dve.tensor_tensor(act_lo[:, b, :], e, act_hi[:, b, :].bitcast(F32), ALU.subtract)\
                    .then_inc(mlo_ready, 1)
            dve.wait_ge(xT_in, 16)
            for b in range(8):
                split_lo(D_O + b + 2)
                dve.wait_ge(dense_mm, D_O + b + 1)
                dve.scalar_tensor_tensor(xT[:, b, :], pm[b % 4][:, :], gt1h[:, b:b + 1], xT[:, b, :],
                                         ALU.mult, ALU.add).then_inc(x2_ready, 1)
            dve.wait_ge(ss2_mm, 1)
            ch.link(dve.tensor_scalar(ss[:, :], pm[0][:, 0:8], 1.0 / D, EPS, ALU.mult, ALU.add))
            rsqrt(ch, dve, ss[:, :], rr[:, :], rt[:, :])
            dve.tensor_tensor(dg0, bc_mid(ident[:, :], NT), bc(rr[:, :], P), ALU.mult).then_inc(diag2_ready, 1)
            dve.wait_ge(rb2_mm, 1)
            for k in range(KT):
                norm_tile(k, xT[:, k, :], gs2[:, k:k + 1], pm[1][:, :], SH2, KT)
            dve.memset(vo[:, 0:1], 0.0).then_inc(po_free, 1)
            dve.memset(vo[:, 1:2], 0.0).then_inc(po_free, 1)

            def ffn_hidden(n, i, ahead=True):
                ds = D_F + 2 * n
                if ahead:
                    split_lo(ds + 2, 2 * i)
                dve.wait_ge(gth_ready, n + 1 + 4 * i)
                ch.link(dve.scalar_tensor_tensor(est[:, 0, :], est[:, 0, :], 1.0, pm[0][:, :], ALU.add, ALU.mult))
                if ahead:
                    split_lo(ds + 3, 2 * i)
                dve.wait_ge(dense_mm, ds + 2 + 8 * i)
                if n >= 2:
                    dve.wait_ge(hhi_ready, n + 4 * i)
                dve.tensor_tensor(est[:, 1, :], est[:, 0, :], pm[1][:, :], ALU.mult).then_inc(gu_read, 1)
                dve.wait_ge(hhi_ready, n + 1 + 4 * i)
                dve.tensor_tensor(h_lo[:, (n // 2) % 2, n % 2, :], est[:, 1, :],
                                  h_hi[:, (n // 2) % 2, n % 2, :].bitcast(F32), ALU.subtract)\
                    .then_inc(hlo_ready, 1)

            def split_o(p, i):
                for e in range(2):
                    dve.wait_ge(ohi_ready, 2 * p + e + 1 + 4 * i)
                    dve.tensor_tensor(o_lo[:, e, :], f_raw[:, e, :], o_hi[:, e, :].bitcast(F32), ALU.subtract)\
                        .then_inc(olo_ready, 1)

            def accumulate(p, i, bs):
                for b in bs:
                    if b == 0:
                        dve.wait_ge(po_free, 8 * p + 2 + 16 * i)
                    dve.wait_ge(o_mm, 8 * p + b + 1 + 16 * i)
                    dve.scalar_tensor_tensor(xT[:, b, :], pm[2 + b % 2][:, :], gt2h[:, b:b + 1], xT[:, b, :],
                                             ALU.mult, ALU.add).then_inc(po_free, 1)

            def ffn_body(n, i, ahead=True):
                split_o(n - 1, i)
                ffn_hidden(2 * n, i)
                accumulate(n - 1, i, range(4))
                ffn_hidden(2 * n + 1, i, ahead)
                accumulate(n - 1, i, range(4, 8))

            ffn_hidden(0, 0)
            ffn_hidden(1, 0)
            base += ch.n
            with dve.Fori(0, 4) as it:
                ch = Chain(dve, vec_chain, it * 4 + base)
                ffn_body(1, it)
                ffn_body(2, it)
                assert ch.n == 4
            base += 16
            ch = Chain(dve, vec_chain, base)
            ffn_body(9, 0)
            ffn_body(10, 0, ahead=False)
            split_o(10, 0)
            accumulate(10, 0, range(8))
            dve.wait_ge(fss_ready, NT)
            ch.link(dve.tensor_scalar(ss[:, :], ss[:, :], 1.0 / D, EPS, ALU.mult, ALU.add))
            rsqrt(ch, dve, ss[:, :], rr[:, :], rt[:, :])
            dve.wait_ge(gbc_in, 16)
            for t in range(NT):
                dve.scalar_tensor_tensor(frow[:, t, :], frow[:, t, :], rr[:, t:t + 1], gbc[:, :],
                                         ALU.mult, ALU.mult).then_inc(row_ready, 1)


_INS = ["x", "c", "w_ada", "b_ada", "norm1_g", "norm2_g", "w_in", "rel_table", "w_conv", "a_log", "dt_bias",
        "gdn_norm_g", "w_branch_a", "w_branch_b", "w_out", "w_ffn_in", "w_ffn_out", "final_g"]


def kernel(**inputs):
    import numpy as _np
    import concourse.bacc as _bacc
    from concourse.bass_utils import run_bass_kernel_spmd as _run

    nc = _bacc.Bacc("TRN2", target_bir_lowering=False, num_devices=1)
    arrays, args = {}, []
    for name in _INS:
        a = _np.asarray(inputs[name])
        if name != "final_g":
            a = a[0]
        if name == "rel_table":
            a = a[:, ::-1]
        a = _np.ascontiguousarray(a)
        arrays[f"in_{name}_dram"] = a
        args.append(nc.dram_tensor(f"in_{name}_dram", a.shape, mybir.dt.from_np(a.dtype), kind="ExternalInput").ap())
    args.append(nc.dram_tensor("out_0_dram", (S, D), F32, kind="ExternalOutput").ap())
    hybrid_layer(nc, *args)
    r = _run(nc, [arrays], core_ids=[0])
    return r.results[0]["out_0_dram"].reshape(1, S, D)
```

```python
from contextlib import ExitStack

import concourse.bass as bass
from concourse import mybir

F32 = mybir.dt.float32
F32R = mybir.dt.float32r
I32 = mybir.dt.int32
ALU = mybir.AluOpType
ACT = mybir.ActivationFunctionType
AX_X = mybir.AxisListType.X

P = 128
S = 1024
D = 1024
KT = D // P
NT = S // P
HALF = S // 2
EPS = 1e-6
NEG = -1e30
A_H, A_D = 8, 64
A_W = A_H * A_D
B_H, B_D = 4, 128
B_W = B_H * B_D
BAND = 5
SCALE = A_D ** -0.5
EXT = 384
F = 2816
FT = F // P
LEVELS = 7

C_QA, C_KA, C_VA = 0, A_W, 2 * A_W
C_QKVB = 3 * A_W
C_Z = C_QKVB + 3 * B_W
C_AB = C_Z + B_W
C_GA = C_AB + 2 * B_H
C_GB = C_GA + D

V_C, V_ADA, V_N1, V_N2, V_NG = 0, 8, 56, 64, 72
V_ROWS = 73
SH1, SC1, GT1, SH2, SC2, GT2 = (8 * n for n in range(6))

NR = 4
ADA_PER = 8
LEAD = 1
RSQRT_MAGIC = float(0x5F3759DF)


class Chain:

    def __init__(self, eng, sem, base=0):
        self.eng, self.sem, self.base, self.n = eng, sem, base, 0

    def link(self, ins):
        ins.then_inc(self.sem, 1)
        self.n += 1
        self.eng.wait_ge(self.sem, self.base + self.n)


def bc(ap, n):
    return ap.unsqueeze(2).broadcast_to([ap.shape[0], ap.shape[1], n])


def bc_mid(ap, n):
    return ap.unsqueeze(1).broadcast_to([ap.shape[0], n, ap.shape[1]])


def heads(ap):
    return ap.rearrange("p (h c) -> p h c", h=B_H)


def rsqrt(ch, eng, v, y, t):
    ch.link(eng.tensor_scalar(t.bitcast(I32), v.bitcast(I32), 1, None, ALU.arith_shift_right))
    ch.link(eng.tensor_scalar(y.bitcast(I32), t.bitcast(I32), -1.0, RSQRT_MAGIC, ALU.mult, ALU.add))
    for _ in range(3):
        ch.link(eng.tensor_tensor(t, y, y, ALU.mult))
        ch.link(eng.scalar_tensor_tensor(t, t, -0.5, v, ALU.mult, ALU.mult))
        ch.link(eng.scalar_tensor_tensor(y, t, 1.5, y, ALU.add, ALU.mult))


RSQRT_LINKS = 11


def hybrid_layer(nc, x, c, w_ada, b_ada, norm1_g, norm2_g, w_in, rel_rev, w_conv, a_log, dt_bias,
                 gdn_norm_g, w_branch_a, w_branch_b, w_out, w_ffn_in, w_ffn_out, final_g, out):
    with ExitStack() as ctx:
        def sbin(stack, name, shape, dt=F32):
            return stack.enter_context(nc.sbuf_tensor(name, shape, dt))

        def psin(stack, name, shape):
            return stack.enter_context(nc.psum_tensor(name, shape, F32))

        def sb(name, shape, dt=F32):
            return sbin(ctx, name, shape, dt)

        def sem(name):
            return ctx.enter_context(nc.semaphore(name))

        def dram(name, shape):
            return nc.dram_tensor(name, shape, F32, kind="Internal").ap()

        xT_d = dram("xT_d", [D, S])
        qkvb_d = dram("qkvb_d", [3 * B_W, S])
        qkva_d = dram("qkva_d", [3 * A_W, S])
        z_d = dram("z_d", [B_W, S])
        ga_d = dram("ga_d", [D, S])
        gb_d = dram("gb_d", [D, S])
        ya_d = dram("ya_d", [A_W, S])
        yb_d = dram("yb_d", [B_W, P + S])
        ext_d = dram("ext_d", [A_H, P * EXT])

        act_hi = sb("act_hi", [P, KT, S], F32R)
        act_lo = sb("act_lo", [P, KT, S], F32R)
        w_raw = sb("w_raw", [P, NR, KT, P])
        w_hi = sb("w_hi", [P, 2, KT, P], F32R)
        w_lo = sb("w_lo", [P, 2, KT, P], F32R)
        est = sb("est", [P, 2, S])
        tmp = sb("tmp", [P, S])
        ident = sb("ident", [P, P])
        ones = sb("ones", [P, P])
        incl = sb("incl", [P, P])
        after = sb("after", [P, P])
        lvl = sb("lvl", [P, LEVELS, P])
        vT = sb("vT", [P, V_ROWS])
        wcT = sb("wcT", [P, 48])
        modT = sb("modT", [P, 48])
        gs = sb("gs", [P, KT])
        gs2 = sb("gs2", [P, KT])
        gt1h = sb("gt1h", [P, KT])
        gt2h = sb("gt2h", [P, KT])
        cs = sb("cs", [P, KT])
        cth = sb("cth", [P, KT])
        ss = sb("ss", [P, NT])
        rr = sb("rr", [P, NT])
        rt = sb("rt", [P, NT])
        ngh = sb("ngh", [P, 1])
        negA = sb("negA", [P, B_H])
        dtb = sb("dtb", [P, B_H])
        ab = sb("ab", [P, NT, 2 * B_H])
        ab2 = sb("ab2", [P, NT, 2 * B_H])
        eab = sb("eab", [P, NT, 2 * B_H])
        beta = sb("beta", [P, NT, B_H])
        g = sb("g", [P, NT, B_H])
        u1 = sb("u1", [P, NT, B_H])
        u2 = sb("u2", [P, NT, B_H])
        u3 = sb("u3", [P, NT, B_H])
        eg = sb("eg", [P, 3, NT, B_H])
        neg_egc = sb("neg_egc", [P, NT, B_H])

        with ExitStack() as st0:
            adab = sbin(st0, "adab", [P, 2, KT, 512])
            asum = sbin(st0, "asum", [P, 2, 512])
            xr = sbin(st0, "xr", [P, 4, D])
            xT0 = sbin(st0, "xT0", [P, KT, S])
            vrow = sbin(st0, "vrow", [V_ROWS + 48, P])
            rrow = sbin(st0, "rrow", [A_H, 257])
            ext = sbin(st0, "ext", [A_H, EXT])
        dg0 = tmp[:, :].rearrange("p (t q) -> p t q", t=NT)
        with ExitStack() as st1:
            def b1(n):
                return sbin(st1, n, [P, B_H * P])
            gst = sbin(st1, "gst", [P, 12, P])
            kd, vn, Ec, Lt, At, gm = (b1(n) for n in ("kd", "vn", "Ec", "Lt", "At", "gm"))
            Tm, Um, Ym, Xm, ym, St, junk = (b1(n) for n in ("Tm", "Um", "Ym", "Xm", "ym", "St", "junk"))
            Ct = sbin(st1, "Ct", [P, 3, B_H * P])
            sskq = sbin(st1, "sskq", [P, 8])
            vkq = sbin(st1, "vkq", [P, 8])
            rkq = sbin(st1, "rkq", [P, 8])
            tkq = sbin(st1, "tkq", [P, 8])
            cj = sbin(st1, "cj", [P, 4])
            cr = sbin(st1, "cr", [P, 4])
            nk = sbin(st1, "nk", [P, 4])
            rq = sbin(st1, "rq", [P, 4])
            sso = sbin(st1, "sso", [P, 4])
            vo = sbin(st1, "vo", [P, 4])
            ro = sbin(st1, "ro", [P, 4])
            to = sbin(st1, "to", [P, 4])
            asc = sbin(st1, "asc", [P, 2, P])
            ast = sbin(st1, "ast", [P, 3, S])
            bias = sbin(st1, "bias", [P, 2, 2 * P])
            Pm = sbin(st1, "Pm", [P, BAND * P])
            PT = sbin(st1, "PT", [P, BAND * P])
            V = sbin(st1, "V", [P, 2, NT, A_D])
            mx = sbin(st1, "mx", [P, 2])
            negm = sbin(st1, "negm", [P, 2])
            psm = sbin(st1, "psm", [P, 2])
            rsm = sbin(st1, "rsm", [P, 2])
            om, on, ybst = b1("om"), b1("on"), b1("ybst")
            yast = sbin(st1, "yast", [P, S])
            a_raw = sbin(st1, "a_raw", [P, 2, KT, P])
        with ExitStack() as st2:
            y_hi = sbin(st2, "y_hi", [P, 8, S], F32R)
            y_lo = sbin(st2, "y_lo", [P, 8, S], F32R)
            gst2 = sbin(st2, "gst2", [P, 2, S])
            yst = sbin(st2, "yst", [P, 4, S])
        with ExitStack() as st3:
            xT = sbin(st3, "xT", [P, KT, S])
            f_raw = sbin(st3, "f_raw", [P, 2, S])
            o_hi = sbin(st3, "o_hi", [P, 2, S], F32R)
            o_lo = sbin(st3, "o_lo", [P, 2, S], F32R)
            h_hi = sbin(st3, "h_hi", [P, 2, 2, S], F32R)
            h_lo = sbin(st3, "h_lo", [P, 2, 2, S], F32R)
        with ExitStack() as st4:
            sbin(st4, "xT_kept", [P, KT, S])
            frow = sbin(st4, "frow", [P, NT, D])
            gbc = sbin(st4, "gbc", [P, D])
        with ExitStack() as pst:
            ps = [psin(pst, f"ps{n}", [P, S]) for n in range(2)]
            aS = psin(pst, "aS", [P, S])
            aT = psin(pst, "aT", [P, HALF])
            gps = psin(pst, "gps", [P, HALF])
        with ExitStack() as pst2:
            pm = [psin(pst2, f"pm{n}", [P, S]) for n in range(4)]

        vec_in, rel_in, misc_in = sem("vec_in"), sem("rel_in"), sem("misc_in")
        ada_in = [sem("ada_in0"), sem("ada_in1")]
        xr_in = [sem(f"xr_in{n}") for n in range(4)]
        cs_ready, row7_ready, rows56_ready = sem("cs_ready"), sem("row7_ready"), sem("rows56_ready")
        consts_ready, ext_ready, ext_stored = sem("consts_ready"), sem("ext_ready"), sem("ext_stored")
        pool_chain, vec_chain, act_chain = sem("pool_chain"), sem("vec_chain"), sem("act_chain")
        vecT_mm, vecT_ready = sem("vecT_mm"), sem("vecT_ready")
        xt_mm, xt_read, xT_stored = sem("xt_mm"), sem("xt_read"), sem("xT_stored")
        ss_ready, diag_ready, rb_mm = sem("ss_ready"), sem("diag_ready"), sem("rb_mm")
        asum_ready, mod_mm, mod_ready = sem("asum_ready"), sem("mod_mm"), sem("mod_ready")
        xn_ready, hi_ready, lo_ready = sem("xn_ready"), sem("hi_ready"), sem("lo_ready")
        raw_in = [sem(f"raw_in{n}") for n in range(NR)]
        wa_in = sem("wa_in")
        whi_ready, wlo_ready, dense_mm = sem("whi_ready"), sem("wlo_ready"), sem("dense_mm")
        est_ready = sem("est_ready")
        est_stored = [sem("est_stored0"), sem("est_stored1")]
        tap_ready, taps_ready, th_ready = sem("tap_ready"), sem("taps_ready"), sem("th_ready")
        ab_read, abT_mm, ab_abs, ab_exp, g_ready, gc_mm, eg_ready = (sem(n) for n in (
            "ab_read", "abT_mm", "ab_abs", "ab_exp", "g_ready", "gc_mm", "eg_ready"))
        gv_in, xm_ready = sem("gv_in"), sem("xm_ready")
        gst_in, gst_free, gdn_mm, gdn_read = sem("gst_in"), sem("gst_free"), sem("gdn_mm"), sem("gdn_read")
        gm_ready, ssk_ready, cj_ready, cr_ready, nk_ready = (sem(n) for n in (
            "gm_ready", "ssk_ready", "cj_ready", "cr_ready", "nk_ready"))
        ec_ready, ct_ready, u0_ready, kd_ready, neg_ready, S_zero = (sem(n) for n in (
            "ec_ready", "ct_ready", "u0_ready", "kd_ready", "neg_ready", "S_zero"))
        sso_ready, on_ready, yb_stored = sem("sso_ready"), sem("on_ready"), sem("yb_stored")
        a_in = [sem("a_in0"), sem("a_in1")]
        asc_ready, adam_mm, ada_all = sem("asc_ready"), sem("adam_mm"), sem("ada_all")
        ast_in = [sem("ast_in0"), sem("ast_in1")]
        ast_free = [sem("ast_free0"), sem("ast_free1")]
        bias_in, bias_free = sem("bias_in"), sem("bias_free")
        sc_mm, negm_ready, exp_ready, pn_ready = (sem(n) for n in ("sc_mm", "negm_ready", "exp_ready", "pn_ready"))
        at_mm, at_read, pv_mm, pv_read, ya_stored = (sem(n) for n in (
            "at_mm", "at_read", "pv_mm", "pv_read", "ya_stored"))
        ya_free, yb_free = sem("ya_free"), sem("yb_free")
        y_in = [sem(f"y_in{n}") for n in range(4)]
        z_in = [sem("z_in0"), sem("z_in1")]
        yz_ready, yhi_ready, ylo_ready = sem("yz_ready"), sem("yhi_ready"), sem("ylo_ready")
        gate_in, merged_ready, pair_free = sem("gate_in"), sem("merged_ready"), sem("pair_free")
        mhi_ready, mlo_ready = sem("mhi_ready"), sem("mlo_ready")
        xT_in, x2_ready, sq_ready, sqs_ready = sem("xT_in"), sem("x2_ready"), sem("sq_ready"), sem("sqs_ready")
        ss2_mm, diag2_ready, rb2_mm = sem("ss2_mm"), sem("diag2_ready"), sem("rb2_mm")
        o_in = [sem("o_in0"), sem("o_in1")]
        ohi_ready, olo_ready, o_mm, po_free = sem("ohi_ready"), sem("olo_ready"), sem("o_mm"), sem("po_free")
        gth_ready, gu_read, hhi_ready, hlo_ready = sem("gth_ready"), sem("gu_read"), sem("hhi_ready"), sem("hlo_ready")
        gbc_in, ft_mm, ss_read = sem("gbc_in"), sem("ft_mm"), sem("ss_read")
        row_ready, out_stored = sem("row_ready"), sem("out_stored")

        D_CONV, D_A, D_B, D_M, D_O, D_F = 5, 13, 29, 45, 53, 61

        def raw_count(ds, i=0):
            return 16 * (ds // NR + 1) + 16 * i

        w_ada_v = w_ada.rearrange("(k p) c -> p k c", p=P)
        w_in_v = w_in.rearrange("(k p) c -> p k c", p=P)
        w_a_v = w_branch_a.rearrange("(k p) c -> p k c", p=P)
        w_b_v = w_branch_b.rearrange("(k p) c -> p k c", p=P)
        w_o_v = w_out.rearrange("(k p) c -> p k c", p=P)
        w_f_v = w_ffn_in.rearrange("(k p) c -> p k c", p=P)

        Q_TK, Q_TQ, Q_TO, Q_D, Q_QS, Q_KS, Q_GK, Q_GQ, Q_TV, Q_T0 = range(10)
        Q_L1 = 10
        Q_Y, Q_AY, Q_KY = range(27, 30)
        NQ = 30
        GSLOT = list(range(1, 31))
        Q_AT = {s: q for q, s in enumerate(GSLOT)}
        SC_AT = [1, 3, 5, 7, 9, 11, 13, 15, 17, 18, 19, 21, 23, 25, 27, 29, 31]
        VT_AT = [1, 16]

        def level_of(q):
            s, part = divmod(q - Q_L1, 3)
            if s == 5 and part == 1:
                part = 2
            return s + 1, part

        def at_index(m=None, e=None):
            if m is None:
                return 8 * e
            return m + 1 if m <= 6 else m + 2

        def fifth(s):
            return ps[(D_B + s // 8 + 1) % 2][:, 0:P]

        def hd(t, h):
            return t[:, h * P:(h + 1) * P]

        def ext_skew(h):
            v = ext_d[bass.ds(h, 1), P - 1:P - 1 + P * (EXT - 1)]
            return v.rearrange("a (p n) -> (a p) n", n=EXT - 1)[:, 0:2 * P]

        block = ctx.enter_context(nc.Block())

        @block.sync
        def _(sp):
            def load_unit(ds, i, view, col):
                if ds >= NR:
                    sp.wait_ge(wlo_ready, ds - NR + 1 + 4 * i)
                sp.dma_start(w_raw[:, ds % NR], view[:, :, bass.ds(col, P)]).then_inc(raw_in[ds % NR], 16)

            for row, v in ((V_C, c), (V_ADA, b_ada), (V_N1, norm1_g), (V_N2, norm2_g), (V_NG, gdn_norm_g)):
                n = v.shape[0] // P
                sp.dma_start(vrow[row:row + n, :], v.rearrange("(r q) -> r q", q=P)).then_inc(vec_in, 16)
            sp.dma_start(vrow[V_ROWS:V_ROWS + 48, :], w_conv.rearrange("t (g q) -> (t g) q", q=P))\
                .then_inc(vec_in, 16)

            def load_x(t):
                if t >= 4:
                    sp.wait_ge(ss_ready, t - 3)
                    sp.wait_ge(xt_mm, t - 3)
                sp.dma_start(xr[:, t % 4, :], x[t * P:(t + 1) * P, :]).then_inc(xr_in[t % 4], 16)

            def load_ada(n):
                if n >= 2:
                    sp.wait_ge(mod_mm, n - 1)
                for e, col in enumerate((SH1 * P, SC1 * P)):
                    sp.dma_start(adab[:, n % 2, :, e * 256:(e + 1) * 256],
                                 w_ada_v[:, :, col + n * 256:col + (n + 1) * 256]).then_inc(ada_in[n % 2], 16)

            for t in range(4):
                load_x(t)
            for t in range(4, NT):
                load_x(t)
            load_ada(0)
            for d in range(2):
                load_unit(d, 0, w_in_v, C_AB if d == 0 else C_QKVB)
            sp.dma_start(rrow[:, :], rel_rev).then_inc(rel_in, 16)
            sp.dma_start(negA[:, :], bass.AP(a_log.tensor, 0, [[0, P], [1, B_H]])).then_inc(misc_in, 16)
            sp.dma_start(dtb[:, :], bass.AP(dt_bias.tensor, 0, [[0, P], [1, B_H]])).then_inc(misc_in, 16)
            for n in range(1, 4):
                load_ada(n)
            for d in range(2, D_A):
                load_unit(d, 0, w_in_v, C_QKVB + (d - 1) * P)
                if d == 5:
                    sp.wait_ge(xt_read, NT)
                    sp.dma_start(xT_d.rearrange("(k p) t -> p k t", p=P), xT0[:, :, :]).then_inc(xT_stored, 16)
                    sp.wait_ge(ext_ready, 1)
                    sp.dma_start(ext_d.rearrange("h (p n) -> h p n", n=EXT),
                                 ext[:, :].unsqueeze(1).broadcast_to([A_H, P, EXT])).then_inc(ext_stored, 16)

            def load_gst(t, groups, landed):
                sp.wait_ge(gst_free, t + LEAD)
                sp.dma_start(gst[:, groups], qkvb_d.rearrange("(g q) t -> q g t", q=P)[:, groups, bass.ds(t * P, P)])\
                    .then_inc(landed, 16)

            with sp.Fori(0, 4) as i:
                for j, col in enumerate((C_QA, C_KA, C_VA, C_Z)):
                    load_unit(D_A + j, i, w_in_v, i * P + col)
                    if j == 0:
                        sp.wait_ge(xT_stored, 16)
                        sp.wait_ge(lo_ready, KT)
                        sp.wait_ge(est_stored[0], 16 * 4)
                        sp.wait_ge(est_stored[1], 16 * 4)
                        load_gst(i, slice(0, 8), gst_in)
                    if j == 1:
                        sp.wait_ge(est_stored[0], 16 * 6)
                        sp.wait_ge(est_stored[1], 16 * 6)
                        load_gst(i, slice(8, 12), gv_in)
                    for a in ((0,), (1, 2), (3, 4), (5, 6, 7))[j]:
                        sp.wait_ge(asc_ready, i * ADA_PER + a + 1)
                        sp.dma_start(a_raw[:, a % 2], w_ada_v[:, :, bass.ds(i * (ADA_PER * P) + (2 * D + a * P), P)])\
                            .then_inc(a_in[a % 2], 16)

            def load_heads(i, e):
                sp.wait_ge(ast_free[e], i + LEAD)
                for n, base in enumerate((C_QA, C_KA, C_VA)):
                    sp.dma_start(ast[e * A_D:(e + 1) * A_D, n, :], qkva_d[bass.ds(i * P + (base + e * A_D), A_D), :])\
                        .then_inc(ast_in[e], 16)

            with sp.Fori(0, 4) as i:
                for j, col in enumerate((C_GA, C_GA + P, C_GB, C_GB + P)):
                    load_unit(D_B + j, i, w_in_v, i * (2 * P) + col)
                load_gst(i + 4, slice(0, 8), gst_in)
                load_gst(i + 4, slice(8, 12), gv_in)
                sp.wait_ge(est_stored[0], 16 * 13)
                sp.wait_ge(est_stored[1], 16 * 14)
                load_heads(i, 0)
                sp.wait_ge(ext_stored, 16)
                sp.wait_ge(bias_free, i + LEAD)
                for e in range(2):
                    sp.dma_start(bias[:, e, :], ext_skew(i * 2 + e)).then_inc(bias_in, 16)
                load_heads(i, 1)

            def load_merge_unit(ds, i):
                sp.wait_ge(wlo_ready, ds - NR + 1 + 4 * i)
                cols = bass.ds(i * (4 * P) + (ds - D_M) * P, P)
                sp.dma_start(w_raw[:, ds % NR, 0:4], w_a_v[:, :, cols]).then_inc(wa_in, 16)
                sp.wait_ge(wa_in, 16 * (ds - D_M + 1))
                sp.dma_start(w_raw[:, ds % NR, 4:8], w_b_v[:, :, cols]).then_inc(raw_in[ds % NR], 16)

            def load_y(k):
                src = ya_d[k * P:(k + 1) * P, :] if k < 4 else yb_d[(k - 4) * P:(k - 3) * P, P:P + S]
                sp.dma_start(yst[:, (k + 1) % 4, :], src).then_inc(y_in[k % 4], 16)

            load_merge_unit(D_M, 0)
            load_merge_unit(D_M + 1, 0)
            for k in range(3):
                sp.wait_ge(ya_stored, 16 * (k + 1))
                load_y(k)
            load_merge_unit(D_M + 2, 0)
            load_merge_unit(D_M + 3, 0)
            sp.wait_ge(ya_stored, 64)
            load_y(3)
            sp.wait_ge(yb_stored, 16 * 9)
            for k in range(4, 8):
                if k >= 6:
                    sp.wait_ge(yz_ready, k - 5)
                sp.dma_start(gst2[:, k % 2, :], z_d[(k - 4) * P:(k - 3) * P, :]).then_inc(z_in[k % 2], 16)
                sp.wait_ge(ylo_ready, k - 3)
                load_y(k)
            sp.wait_ge(est_stored[0], 16 * 22)
            sp.wait_ge(est_stored[1], 16 * 22)

            def load_gates(b):
                if b == 0:
                    sp.wait_ge(yz_ready, 4)
                sp.wait_ge(pair_free, b + 2)
                for n, t in enumerate((ga_d, gb_d)):
                    sp.dma_start(gst2[:, n, :], t[bass.ds(b * P, P), :]).then_inc(gate_in, 16)

            for b in range(4):
                load_gates(b)
                load_merge_unit(D_M + 4 + b, 0)
            for b in range(4, 8):
                load_gates(b)
                load_unit(D_O + b - 4, 0, w_o_v, (b - 4) * P)
            sp.wait_ge(dense_mm, D_O)
            sp.wait_ge(pair_free, 10)
            sp.dma_start(xT[:, :, :], xT_d.rearrange("(k p) t -> p k t", p=P)).then_inc(xT_in, 16)
            for b in range(4, 8):
                load_unit(D_O + b, 0, w_o_v, b * P)

            def load_pair(ds, i, col):
                load_unit(ds, i, w_f_v, col)
                load_unit(ds + 1, i, w_f_v, col + F)

            def load_o(n, i):
                for e in range(2):
                    if n >= 2:
                        sp.wait_ge(olo_ready, n - 1 + e + 4 * i)
                    sp.dma_start(f_raw[:, e, :], w_ffn_out[bass.ds(i * (4 * P) + (n + e) * P, P), :])\
                        .then_inc(o_in[e], 16)

            load_pair(D_F, 0, 0)
            load_pair(D_F + 2, 0, P)
            load_o(0, 0)

            def load_body(n, i):
                load_pair(D_F + 4 * n, i * 2, i * (4 * P) + 2 * n * P)
                load_pair(D_F + 4 * n + 2, i * 2, i * (4 * P) + (2 * n + 1) * P)
                load_o(2 * n, i)

            load_body(1, 0)
            with sp.Fori(0, 4) as it:
                load_body(2, it)
                load_body(3, it)
            load_body(10, 0)
            sp.wait_ge(o_mm, 8 * 11 + LEAD)
            sp.dma_start(gbc[:, :], bass.AP(final_g.tensor, 0, [[0, P], [1, D]])).then_inc(gbc_in, 16)
            for t in range(NT):
                sp.wait_ge(row_ready, t + 1)
                sp.dma_start(out[t * P:(t + 1) * P, :], frow[:, t, :]).then_inc(out_stored, 16)
            sp.wait_ge(out_stored, 16 * NT)

        @block.gpsimd
        def _(pool):
            for s in (yb_free, ya_free):
                pool.sem_inc(s, LEAD)
            ch = Chain(pool, pool_chain)
            pool.memset(ident[:, :], 0.0).then_inc(pool_chain, 1)
            pool.memset(ones[:, :], 1.0).then_inc(pool_chain, 1)
            pool.memset(incl[:, :], 1.0).then_inc(pool_chain, 1)
            pool.memset(after[:, :], 1.0).then_inc(pool_chain, 1)
            pool.memset(lvl[:, :, :], 0.0).then_inc(pool_chain, 1)
            pool.memset(ext[:, :], 0.0).then_inc(pool_chain, 1)
            ch.n = 6
            pool.wait_ge(pool_chain, 6)
            pool.affine_select(out=ident[:, :], in_=ident[:, :], compare_op=ALU.not_equal, fill=1.0,
                               base=0, pattern=[[-1, P]], channel_multiplier=1).then_inc(consts_ready, 1)
            pool.affine_select(out=incl[:, :], in_=incl[:, :], compare_op=ALU.is_ge, fill=0.0,
                               base=0, pattern=[[1, P]], channel_multiplier=-1).then_inc(consts_ready, 1)
            pool.affine_select(out=after[:, :], in_=after[:, :], compare_op=ALU.is_ge, fill=0.0,
                               base=-1, pattern=[[-1, P]], channel_multiplier=1).then_inc(consts_ready, 1)
            pool.wait_ge(cs_ready, 1)
            for n in range(4):
                pool.wait_ge(ada_in[n % 2], 32 * (n // 2 + 1))
                pool.tensor_scalar(adab[:, n % 2, 7, :], adab[:, n % 2, 7, :], cs[:, 7:8], None, ALU.mult)\
                    .then_inc(row7_ready, 1)
            for s in range(LEVELS):
                b = 1 << s
                odd = lvl[:, s, :].rearrange("p (n two b) -> p n two b", two=2, b=b)[:, :, 1, :]
                nb = P // (2 * b)
                ch.link(pool.memset(odd, 1.0))
                ch.link(pool.affine_select(out=odd, in_=odd, compare_op=ALU.is_ge, fill=0.0, base=0,
                                           pattern=[[-2 * b, nb], [0, b]], channel_multiplier=1))
                ch.link(pool.affine_select(out=odd, in_=odd, compare_op=ALU.is_ge, fill=0.0, base=b - 1,
                                           pattern=[[2 * b, nb], [0, b]], channel_multiplier=-1))
            pool.wait_ge(rel_in, 16)
            pool.tensor_scalar(ext[:, P - 1:EXT], rrow[:, :], rrow[:, 0:1], 1.0 / SCALE,
                               ALU.subtract, ALU.mult).then_inc(ext_ready, 1)

            def wait_apart(s, value):
                value = pool.to_reg(value)
                pool.wait_ge(ext_ready, 1)
                pool.wait_ge(s, value)

            def store(ds, i, dst):
                if ds < D_CONV:
                    pool.wait_ge(est_ready, ds)
                else:
                    wait_apart(est_ready, ds + 4 * i)
                pool.dma_start(dst, est[:, ds % 2, :]).then_inc(est_stored[ds % 2], 16)

            for d in range(1, D_CONV):
                store(d, 0, qkvb_d[(d - 1) * P:d * P, :])
            pool.wait_ge(lo_ready, KT)
            pool.wait_ge(xT_stored, 16)
            pool.memset(St[:, :], 0.0).then_inc(S_zero, 1)
            pool.memset(on[:, :], 0.0).then_inc(on_ready, 1)
            with pool.Fori(0, 2) as i:
                for j in range(4):
                    store(D_CONV + j, i, qkvb_d[bass.ds(i * (4 * P) + (D_CONV + j - 1) * P, P), :])

            def gdn_slot(t, s):
                if s == 0:
                    pool.wait_ge(eg_ready, 1)
                    pool.wait_ge(gdn_mm, t * NQ + LEAD)
                    pool.tensor_tensor(heads(gm[:, :]), bc_mid(incl[:, :], B_H), bc(g_of(t), P), ALU.mult)\
                        .then_inc(gm_ready, 1)
                q = Q_AT.get(s)
                if q == Q_TO:
                    wait_apart(gdn_read, t * NQ + Q_TO + 1 + LEAD)
                    pool.dma_start(yb_d.rearrange("(h q) t -> q h t", q=P)[:, :, bass.ds(t * P, P)],
                                   heads(ybst[:, :])).then_inc(yb_stored, 16)
                if q == Q_QS:
                    pool.wait_ge(gdn_read, t * NQ + Q_D + 1 + LEAD)
                    ch.link(pool.tensor_tensor(heads(Ec[:, :]), heads(Ec[:, :]), bc_mid(incl[:, :], B_H), ALU.mult))
                    pool.wait_ge(cj_ready, t + 1)
                    pool.tensor_tensor(heads(Ec[:, :]), heads(Ec[:, :]), bc(cj[:, :], P), ALU.mult)\
                        .then_inc(ec_ready, 1)
                if q == Q_GQ:
                    pool.wait_ge(gdn_read, t * NQ + Q_GK + 1 + LEAD)
                    for s_ in range(3):
                        pool.tensor_tensor(heads(Ct[:, s_, :]), heads(Lt[:, :]), bc_mid(lvl[:, s_, :], B_H),
                                           ALU.mult).then_inc(ct_ready, 1)
                if q == Q_L1:
                    pool.wait_ge(u0_ready, t + 1)
                    pool.tensor_tensor(heads(Ct[:, 0, :]), heads(Lt[:, :]), bc_mid(lvl[:, 3, :], B_H),
                                       ALU.mult).then_inc(ct_ready, 1)
                if q == Q_L1 + 9:
                    pool.wait_ge(yb_stored, t * 16 + 16)
                    pool.sem_inc(yb_free, 1)
                    pool.wait_ge(cr_ready, t + 1)
                    pool.wait_ge(ssk_ready, t * B_H + B_H)
                    pool.tensor_tensor(heads(kd[:, :]), heads(kd[:, :]), bc(cr[:, :], P), ALU.mult)\
                        .then_inc(kd_ready, 1)
                    pool.wait_ge(nk_ready, t + 1)
                    pool.wait_ge(gdn_read, t * NQ + Q_TV + 1 + LEAD)
                    ch.link(pool.tensor_tensor(heads(vn[:, :]), heads(vn[:, :]), bc(nk[:, :], P), ALU.mult))
                    pool.tensor_tensor(Xm[:, :], Xm[:, :], vn[:, :], ALU.add).then_inc(xm_ready, 1)
                for lv in (4, 5, 6):
                    if q == Q_L1 + 3 * (lv - 4) + 1:
                        pool.wait_ge(gdn_mm, t * NQ + Q_L1 + 3 * (lv - 4) + 1 + LEAD)
                        pool.tensor_tensor(heads(Ct[:, lv % 3, :]), heads(Lt[:, :]), bc_mid(lvl[:, lv, :], B_H),
                                           ALU.mult).then_inc(ct_ready, 1)

            def g_of(t):
                return g[:, bass.ds(t, 1), :].rearrange("p a h -> p (a h)")

            pool_base = ch.n
            with pool.Fori(0, 4) as i:
                ch = Chain(pool, pool_chain, i * 2 + pool_base)
                for s in range(32):
                    gdn_slot(i, s)
                    if s in (13, 21, 29):
                        j = s // 8 - 1
                        store(D_A + j, i, qkva_d[bass.ds(i * P + j * A_W, P), :])
                store(D_A + 3, i, z_d[bass.ds(i * P, P), :])
                assert ch.n == 2
            pool_base += 8
            with pool.Fori(0, 4) as i:
                ch = Chain(pool, pool_chain, i * 2 + pool_base)
                for s in range(32):
                    gdn_slot(i + 4, s)
                    if s in (13, 21, 29):
                        j = s // 8 - 1
                        store(D_B + j, i, (ga_d, ga_d, gb_d)[j][bass.ds(i * (2 * P) + (0, P, 0)[j], P), :])
                wait_apart(pv_read, i * 16 + 16 + LEAD)
                pool.dma_start(ya_d[bass.ds(i * P, P), :], yast[:, :]).then_inc(ya_stored, 16)
                store(D_B + 3, i, gb_d[bass.ds(i * (2 * P) + P, P), :])
                pool.wait_ge(ya_stored, i * 16 + 16)
                pool.sem_inc(ya_free, 1)
            pool.wait_ge(gdn_read, NT * NQ + 1 + LEAD)
            pool.dma_start(yb_d.rearrange("(h q) t -> q h t", q=P)[:, :, S:S + P], heads(ybst[:, :]))\
                .then_inc(yb_stored, 16)

        @block.tensor
        def _(pe):
            for s in (gst_free, adam_mm, ast_free[0], ast_free[1], gdn_mm, o_mm):
                pe.sem_inc(s, LEAD)
            def dense_k(ds, k, dst, hi, lo, first, last):
                for n, (wt, at) in enumerate(((w_hi, hi), (w_hi, lo), (w_lo, hi))):
                    for h in range(2):
                        cols = slice(h * HALF, (h + 1) * HALF)
                        ins = pe.matmul(dst[:, cols], wt[:, ds % 2, k, :], at[:, cols],
                                        start=(first and n == 0), stop=(last and n == 2))
                return ins

            def unit_k(ds, i, k, dst):
                if k == 0:
                    pe.wait_ge(wlo_ready, ds + 1 + 4 * i)
                    if ds >= 3:
                        pe.wait_ge(est_ready, ds - 2 + 4 * i)
                    elif ds == 2:
                        pe.wait_ge(ab_read, 1)
                ins = dense_k(ds, k, dst, act_hi[:, k, :], act_lo[:, k, :], k == 0, k == KT - 1)
                if k == KT - 1:
                    ins.then_inc(dense_mm, 1)

            def in_step(k0, k1):
                steps = [(d, k) for k in range(k0, min(k1, 6)) for d in range(2)]
                return steps + [(d, k) for d in range(2) for k in range(max(k0, 6), k1)]

            def units01(n):
                for d, k in in_step(2 * n, 2 * n + 2):
                    if d == 0:
                        pe.wait_ge(lo_ready, k + 1)
                    ins = dense_k(d, k, ps[d], act_hi[:, k, :], act_lo[:, k, :], k == 0, k == 7)
                    if k == 7:
                        ins.then_inc(dense_mm, 1)

            pe.wait_ge(consts_ready, 3)
            pe.wait_ge(vec_in, 16 * 6)
            n = V_ROWS + 48
            pe.transpose(gps[:, 0:n], vrow[:, :], ident[0:n, 0:n]).then_inc(vecT_mm, 1)
            for t in range(NT):
                pe.wait_ge(xr_in[t % 4], 16 * (t // 4 + 1))
                if t >= 2:
                    pe.wait_ge(xt_read, t - 1)
                for k in range(KT):
                    ins = pe.transpose(ps[t % 2][:, k * P:(k + 1) * P], xr[:, t % 4, k * P:(k + 1) * P],
                                       ident[:, :])
                ins.then_inc(xt_mm, 1)
            pe.wait_ge(diag_ready, 1)
            for t in range(NT):
                ins = pe.matmul(aS[:, t * P:(t + 1) * P], ones[:, :], dg0[:, t, :], start=True, stop=True)
            ins.then_inc(rb_mm, 1)
            pe.wait_ge(vecT_ready, 2)
            pe.wait_ge(xt_read, NT)
            pe.wait_ge(wlo_ready, 2)
            for n in range(4):
                pe.wait_ge(asum_ready, n + 1)
                pe.wait_ge(row7_ready, n + 1)
                pe.wait_ge(rows56_ready, 2 * n + 2)
                if n:
                    pe.wait_ge(mod_ready, n)
                for q in range(4):
                    col = 8 * (q // 2) + 2 * n + q % 2
                    pe.matmul(gps[:, col:col + 1], asum[:, n % 2, q * P:(q + 1) * P], ones[:, 0:1],
                              start=True, stop=False)
                    for k in (5, 6, 7):
                        ins = pe.matmul(gps[:, col:col + 1], adab[:, n % 2, k, q * P:(q + 1) * P], ones[:, 0:1],
                                        start=False, stop=(k == 7))
                ins.then_inc(mod_mm, 1)
                if n:
                    units01(n - 1)
            units01(3)
            for d in range(2, D_CONV):
                for k in range(KT):
                    unit_k(d, 0, k, ps[d % 2])
                if d == 2:
                    pe.wait_ge(ab_read, 1)
                    pe.wait_ge(mod_ready, 1)
                    for t in range(NT):
                        ins = pe.transpose(gps[:, t * 8:(t + 1) * 8], est[0:8, 0, t * P:(t + 1) * P],
                                           ident[0:8, 0:8])
                    ins.then_inc(abT_mm, 1)
            with pe.Fori(0, 2) as i:
                for j in range(4):
                    for k in range(KT):
                        unit_k(D_CONV + j, i, k, ps[(D_CONV + j) % 2])
            pe.wait_ge(g_ready, 1)
            for n, m in enumerate((incl, after, ones)):
                ins = pe.matmul(aS[:, HALF + n * 32:HALF + (n + 1) * 32], m[:, :],
                                g[:, :, :].rearrange("p t h -> p (t h)"), start=True, stop=True)
            ins.then_inc(gc_mm, 1)
            pe.wait_ge(S_zero, 1)

            def gdn_step(t, q, order=None):
                order = q if order is None else order
                pe.wait_ge(gdn_read, t * NQ + order + LEAD)
                if q == Q_TO:
                    pe.wait_ge(on_ready, t + 1)
                    for h in range(B_H):
                        ins = pe.transpose(hd(gps, h), hd(on, h), ident[:, :])
                elif q in (Q_TK, Q_TQ, Q_TV):
                    if q != Q_TQ:
                        pe.wait_ge(gst_in if q == Q_TK else gv_in, t * 16 + 16)
                    base = {Q_TQ: 0, Q_TK: 4, Q_TV: 8}[q]
                    for h in range(B_H):
                        ins = pe.transpose(hd(gps, h), gst[:, base + h, :], ident[:, :])
                elif q == Q_D:
                    pe.wait_ge(gm_ready, t + 1)
                    ins = pe.matmul(gps[:, :], after[:, :], gm[:, :], start=True, stop=True)
                elif q in (Q_QS, Q_KS):
                    for h in range(B_H):
                        ins = pe.matmul(hd(gps, h), gst[:, (0 if q == Q_QS else 4) + h, :], hd(St, h),
                                        start=True, stop=True)
                elif q in (Q_GK, Q_GQ):
                    for h in range(B_H):
                        ins = pe.matmul(hd(gps, h), gst[:, 4 + h, :], gst[:, (4 if q == Q_GK else 0) + h, :],
                                        start=True, stop=True)
                elif q == Q_T0:
                    pe.wait_ge(u0_ready, t + 1)
                    for h in range(B_H):
                        ins = pe.transpose(hd(gps, h), hd(Um, h), ident[:, :])
                        if h == 0:
                            ins.then_inc(gst_free, 1)
                elif q == Q_Y:
                    pe.wait_ge(xm_ready, t + 1)
                    for h in range(B_H):
                        ins = pe.matmul(hd(gps, h), hd(Um, h), hd(Xm, h), start=True, stop=True)
                elif q == Q_AY:
                    for h in range(B_H):
                        ins = pe.matmul(hd(gps, h), hd(At, h), hd(ym, h), start=True, stop=True)
                elif q == Q_KY:
                    pe.wait_ge(kd_ready, t + 1)
                    for h in range(B_H):
                        ins = pe.matmul(hd(gps, h), hd(kd, h), hd(ym, h), start=True, stop=True)
                else:
                    lv, part = level_of(q)
                    for h in range(B_H):
                        if part == 0:
                            if h == 0:
                                pe.wait_ge(ct_ready, t * LEVELS + lv + 1)
                            ins = pe.matmul(hd(gps, h), Ct[:, lv % 3, h * P:(h + 1) * P], hd(Tm, h),
                                            start=True, stop=True)
                        elif part == 1:
                            ins = pe.matmul(hd(gps, h), hd(Um, h), hd(Ym, h), start=True, stop=True)
                        elif lv < LEVELS - 1:
                            ins = pe.transpose(hd(gps, h), hd(Tm, h), ident[:, :])
                        else:
                            ins = pe.matmul(hd(gps, h), hd(Ym, h), hd(Um, h), start=True, stop=True)
                ins.then_inc(gdn_mm, 1)

            with pe.Fori(0, 4) as i:
                for s in range(32):
                    if s in Q_AT:
                        gdn_step(i, Q_AT[s])
                    unit_k(D_A + s // 8, i, s % 8, ps[(D_A + s // 8) % 2])
                    if s % 4 == 3:
                        a = s // 4
                        pe.wait_ge(asc_ready, i * ADA_PER + a + 3)
                        pe.matmul(aS[:, bass.ds(i * ADA_PER + a, 1)], asc[:, a % 2, :], ones[:, 0:1],
                                  start=True, stop=True).then_inc(adam_mm, 1)
            def attention_slot(i, s):
                for m in range(16):
                    e, qt = divmod(m, NT)
                    nk_ = min(BAND, qt + 1)
                    rows = slice(e * A_D, (e + 1) * A_D)
                    if s == SC_AT[m + 1] + 1:
                        pe.wait_ge(at_read, i * 18 + at_index(m=m) + 1 + LEAD)
                        for kt in range(nk_):
                            ins = pe.matmul(aT[0:A_D, 0:P], V[:, e, qt - nk_ + 1 + kt, :],
                                            PT[:, kt * P:(kt + 1) * P], start=(kt == 0), stop=(kt == nk_ - 1))
                        ins.then_inc(pv_mm, 1)
                    if s == SC_AT[m + 1]:
                        pe.wait_ge(pn_ready, i * 16 + m + 1)
                        pe.wait_ge(at_read, i * 18 + at_index(m=m) + LEAD)
                        pe.wait_ge(pv_read, i * 16 + m + LEAD)
                        if nk_ == BAND:
                            pe.wait_ge(est_ready, D_B + s // 8 - 1 + 4 * i)
                        for kt in range(nk_):
                            dst = aT[:, kt * P:(kt + 1) * P] if kt < 4 else fifth(s)
                            ins = pe.transpose(dst, Pm[:, kt * P:(kt + 1) * P], ident[:, :])
                            if kt == 0 and m % 8 == 7:
                                ins.then_inc(ast_free[e], 1)
                        ins.then_inc(at_mm, 1)
                    if s == SC_AT[m]:
                        pe.wait_ge(exp_ready, i * 16 + m + LEAD)
                        if m == 0:
                            pe.wait_ge(ada_all, 1)
                        if m % NT == 0:
                            pe.wait_ge(ast_in[e], i * 48 + 48)
                        k0 = (qt - nk_ + 1) * P
                        w = nk_ * P
                        ins = pe.matmul(aS[:, 0:min(w, 512)], ast[rows, 0, qt * P:(qt + 1) * P],
                                        ast[rows, 1, k0:k0 + min(w, 512)], start=True, stop=True)
                        if w > 512:
                            ins = pe.matmul(aS[:, 512:w], ast[rows, 0, qt * P:(qt + 1) * P],
                                            ast[rows, 1, k0 + 512:k0 + w], start=True, stop=True)
                        ins.then_inc(sc_mm, 1)
                for e in range(2):
                    if s == VT_AT[e]:
                        landed = pe.to_reg(i * 48 + 48)
                        copied = pe.to_reg(i * 18 + at_index(e=e) + LEAD)
                        yT_read = pe.to_reg(i * 16 + 7 * e + LEAD)
                        pe.wait_ge(ada_all, 1)
                        pe.wait_ge(ast_in[e], landed)
                        pe.wait_ge(at_read, copied)
                        pe.wait_ge(pv_read, yT_read)
                        rows = slice(e * A_D, (e + 1) * A_D)
                        for kt in range(NT):
                            ins = pe.transpose(aT[:, kt * A_D:(kt + 1) * A_D], ast[rows, 2, kt * P:(kt + 1) * P],
                                               ident[rows, rows])
                        ins.then_inc(at_mm, 1)

            with pe.Fori(0, 4) as i:
                for s in range(32):
                    attention_slot(i, s)
                    if s in Q_AT:
                        gdn_step(i + 4, Q_AT[s])
                    unit_k(D_B + s // 8, i, s % 8, ps[(D_B + s // 8) % 2])
                attention_slot(i, 32)
            gdn_step(NT, Q_TO, 0)

            pe.wait_ge(pair_free, 2)
            def merge_k(b, k):
                ins = dense_k(D_M + b, k, pm[2 * (b % 2) + k // 4], y_hi[:, k, :], y_lo[:, k, :],
                              k % 4 == 0, k % 4 == 3)
                if k == 7:
                    ins.then_inc(dense_mm, 1)

            pe.wait_ge(wlo_ready, D_M + 2)
            for b, k in in_step(0, 8):
                pe.wait_ge(ylo_ready, k + 1)
                merge_k(b, k)
            for b in range(2, 8):
                d = D_M + b
                pe.wait_ge(wlo_ready, d + 1)
                pe.wait_ge(pair_free, b + 1)
                for k in range(8):
                    merge_k(b, k)
            for b in range(8):
                d = D_O + b
                pe.wait_ge(wlo_ready, d + 1)
                if b == 0:
                    pe.wait_ge(pair_free, 9)
                if b >= 4:
                    pe.wait_ge(x2_ready, b - 3)
                for k in range(8):
                    if b == 0:
                        pe.wait_ge(mlo_ready, k + 1)
                    ins = dense_k(d, k, pm[b % 4], act_hi[:, k, :], act_lo[:, k, :], k == 0, k == 7)
                ins.then_inc(dense_mm, 1)
            def token_sums(norm):
                for n, (count, src) in enumerate(((None, tmp[:, :]), (8 * norm + 8, est[:, 1, :]))):
                    if count is None:
                        pe.wait_ge(sqs_ready, 6 * norm + 6)
                    else:
                        pe.wait_ge(sq_ready, count)
                    for t in range(NT):
                        ins = pe.matmul(pm[0][:, n * 8 + t:n * 8 + t + 1], src[:, t * P:(t + 1) * P], ones[:, 0:1],
                                        start=True, stop=True)
                ins.then_inc(ss2_mm, 1)

            token_sums(0)
            pe.wait_ge(x2_ready, 8)
            pe.wait_ge(diag2_ready, 1)
            for t in range(NT):
                ins = pe.matmul(pm[3][:, t * P:(t + 1) * P], ones[:, :], dg0[:, t, :], start=True, stop=True)
            ins.then_inc(rb2_mm, 1)

            def gate_up(n, i, read=None):
                for e in range(2):
                    ds = D_F + 2 * n + e
                    pe.wait_ge(wlo_ready, ds + 1 + 8 * i)
                    if e == 0 and n > 1:
                        pe.wait_ge(gu_read, n + 4 * i if read is None else read)
                    for k in range(KT):
                        ins = dense_k(ds, k, pm[e + (2 if n == 1 else 0)], act_hi[:, k, :], act_lo[:, k, :],
                                      k == 0, k == 7)
                    ins.then_inc(dense_mm, 1)

            def ffn_out(p, i, bs):
                for b in bs:
                    if b == 0:
                        pe.wait_ge(hlo_ready, 2 * p + 2 + 4 * i)
                        pe.wait_ge(olo_ready, 2 * p + 2 + 4 * i)
                    pe.wait_ge(po_free, 8 * p + b + 1 + 16 * i)
                    dst = pm[2 + b % 2]
                    for e in range(2):
                        for n, (wt, at) in enumerate(((o_hi, h_hi), (o_hi, h_lo), (o_lo, h_hi))):
                            for h in range(2):
                                cols = slice(h * HALF, (h + 1) * HALF)
                                ins = pe.matmul(dst[:, cols], wt[:, e, b * P:(b + 1) * P], at[:, p % 2, e, cols],
                                                start=(e == 0 and n == 0), stop=(e == 1 and n == 2))
                    ins.then_inc(o_mm, 1)

            def ffn_body(n, i, read=None):
                gate_up(2 * n, i, read)
                ffn_out(n - 1, i, range(4))
                gate_up(2 * n + 1, i)
                ffn_out(n - 1, i, range(4, 8))

            pe.wait_ge(wlo_ready, D_F + 2)
            for e, k in in_step(0, KT):
                pe.wait_ge(lo_ready, KT + k + 1)
                ins = dense_k(D_F + e, k, pm[e], act_hi[:, k, :], act_lo[:, k, :], k == 0, k == 7)
                if k == 7:
                    ins.then_inc(dense_mm, 1)
            gate_up(1, 0)
            ffn_body(1, 0, read=1)
            with pe.Fori(0, 4) as it:
                ffn_body(2, it)
                ffn_body(3, it)
            ffn_body(10, 0)
            ffn_out(10, 0, range(8))
            token_sums(1)
            for t in range(NT):
                if t >= 4:
                    pe.wait_ge(row_ready, t - 3)
                if t == 0:
                    pe.wait_ge(po_free, 8 * 11 + 2)
                if t == 3:
                    pe.wait_ge(ss_read, 2)
                for k in range(KT):
                    ins = pe.transpose(pm[(t + 1) % 4][:, k * P:(k + 1) * P], xT[:, k, t * P:(t + 1) * P], ident[:, :])
                ins.then_inc(ft_mm, 1)

        @block.scalar
        def _(act):
            for s in (gdn_read, exp_ready, pv_read, at_read):
                act.sem_inc(s, LEAD)
            def split_hi(ds, i=0):
                act.wait_ge(raw_in[ds % NR], raw_count(ds, i))
                if ds >= 2:
                    act.wait_ge(dense_mm, ds - 1 + 4 * i)
                act.activation(w_hi[:, ds % 2], w_raw[:, ds % NR], ACT.Copy).then_inc(whi_ready, 1)

            act.wait_ge(vecT_mm, 1)
            act.activation(vT[:, :], gps[:, 0:V_ROWS], ACT.Copy).then_inc(vecT_ready, 1)
            act.wait_ge(vecT_ready, 1)
            act.activation(cth[:, :], vT[:, V_C:V_C + 8], ACT.Tanh, scale=0.5).then_inc(act_chain, 1)
            act.activation(wcT[:, :], gps[:, V_ROWS:V_ROWS + 48], ACT.Copy, scale=0.5).then_inc(vecT_ready, 1)
            act.activation(ngh[:, :], vT[:, V_NG:V_NG + 1], ACT.Copy, scale=0.5).then_inc(act_chain, 1)
            for t in range(NT):
                act.wait_ge(xr_in[t % 4], 16 * (t // 4 + 1))
                if t:
                    act.wait_ge(ss_ready, t)
                act.activation(tmp[:, :], xr[:, t % 4, :], ACT.Square, accum_out=ss[:, t:t + 1])\
                    .then_inc(ss_ready, 1)
            def ada_rows(n):
                act.wait_ge(ada_in[n % 2], 32 * (n // 2 + 1))
                for k in (5, 6):
                    act.activation(adab[:, n % 2, k, :], adab[:, n % 2, k, :], ACT.Copy, scale=cs[:, k:k + 1])\
                        .then_inc(rows56_ready, 1)

            act.wait_ge(cs_ready, 1)
            ada_rows(0)
            act.wait_ge(misc_in, 32)
            act.activation(negA[:, :], negA[:, :], ACT.Exp).then_inc(act_chain, 1)
            split_hi(0)
            split_hi(1)
            for n in range(4):
                if n < 3:
                    ada_rows(n + 1)
                for k in (2 * n, 2 * n + 1):
                    act.wait_ge(xn_ready, k + 1)
                    act.activation(act_hi[:, k, :], est[:, k % 2, :], ACT.Identity,
                                   bias=modT[:, SH1 + k:SH1 + k + 1]).then_inc(hi_ready, 1)

            def evac_conv(ds, i, col):
                act.wait_ge(dense_mm, ds + 1 + 4 * i)
                act.wait_ge(est_ready, ds - 1 + 4 * i)
                if ds >= 3:
                    act.wait_ge(est_stored[ds % 2], 16 * ((ds - 1) // 2) + 32 * i)
                act.activation(est[:, ds % 2, :], ps[ds % 2][:, :], ACT.Copy, scale=col).then_inc(tap_ready, 1)
                split_hi(ds + 2, i)
                act.wait_ge(taps_ready, ds + 4 * i)
                act.activation(tmp[:, :], est[:, ds % 2, :], ACT.Tanh).then_inc(th_ready, 1)

            for d in range(D_CONV):
                if d == 0:
                    split_hi(2)
                    act.wait_ge(lo_ready, KT)
                    act.activation(est[0:8, 0, :], ps[0][0:8, :], ACT.Copy).then_inc(ab_read, 1)
                    continue
                if d == 2:
                    act.wait_ge(abT_mm, 1)
                evac_conv(d, 0, wcT[:, 36 + d - 1:36 + d])
                if d == 3:
                    act.wait_ge(ab_abs, 1)
                    act.activation(eab[:, :, :], eab[:, :, :], ACT.Exp, scale=-1.0).then_inc(ab_exp, 1)
            with act.Fori(0, 2) as i:
                for j in range(4):
                    evac_conv(D_CONV + j, i, wcT[:, bass.ds(i * 4 + (36 + D_CONV + j - 1), 1)])
            act.wait_ge(gc_mm, 1)
            act.activation(eg[:, :, :, :].rearrange("p a t h -> p (a t h)"), aS[:, HALF:HALF + 96], ACT.Exp)\
                .then_inc(eg_ready, 1)

            def gdn_read_act(t, q, order=None):
                lv = part = None
                if Q_L1 <= q < Q_Y:
                    lv, part = level_of(q)
                copies = {Q_TK: kd, Q_TV: vn, Q_T0: Tm, Q_Y: ym}
                dst = copies.get(q)
                if part == 0:
                    dst = Ym
                if part == 2 and lv < LEVELS - 1:
                    dst = Um
                if dst is not None:
                    act.wait_ge(gdn_mm, t * NQ + q + 1 + LEAD)
                    act.activation(dst[:, :], gps[:, :], ACT.Copy).then_inc(gdn_read, 1)
                if q == Q_TO:
                    act.wait_ge(gdn_mm, t * NQ + (q if order is None else order) + 1 + LEAD)
                    act.wait_ge(yb_free, t + LEAD)
                    act.activation(ybst[:, :], gps[:, :], ACT.Copy, scale=ngh[:, :]).then_inc(gdn_read, 1)
                if q == Q_TQ:
                    act.wait_ge(gdn_mm, t * NQ + q + 1 + LEAD)
                    for h in range(B_H):
                        ins = act.activation(hd(junk, h), hd(gps, h), ACT.Square, accum_out=sskq[:, 4 + h:5 + h])
                    ins.then_inc(gdn_read, 1)
                    act.wait_ge(gdn_read, t * NQ + q + 1 + LEAD)
                    for h in range(B_H):
                        act.activation(hd(junk, h), hd(kd, h), ACT.Square, accum_out=sskq[:, h:h + 1])\
                            .then_inc(ssk_ready, 1)
                if q == Q_D:
                    act.wait_ge(gdn_mm, t * NQ + q + 1 + LEAD)
                    act.activation(Ec[:, :], gps[:, :], ACT.Exp).then_inc(gdn_read, 1)
                if q == Q_KY:
                    act.wait_ge(gdn_read, t * NQ + Q_AY + 1 + LEAD)
                    for h in range(B_H):
                        act.activation(hd(junk, h), hd(om, h), ACT.Square, accum_out=sso[:, h:h + 1])\
                            .then_inc(sso_ready, 1)

            def evac(ds, i, kind):
                act.wait_ge(dense_mm, ds + 1 + 4 * i)
                act.wait_ge(est_ready, ds - 1 + 4 * i)
                if kind == "z":
                    act.activation(tmp[:, :], ps[ds % 2][:, :], ACT.Tanh, scale=0.5).then_inc(th_ready, 1)
                else:
                    act.wait_ge(est_stored[ds % 2], 16 * ((ds - 1) // 2) + 32 * i)
                    if kind == "copy":
                        act.activation(est[:, ds % 2, :], ps[ds % 2][:, :], ACT.Copy).then_inc(est_ready, 1)
                    else:
                        act.activation(est[:, ds % 2, :], ps[ds % 2][:, :], ACT.Tanh, scale=0.5)\
                            .then_inc(est_ready, 1)
                split_hi(ds + 2, i)

            with act.Fori(0, 4) as i:
                for s in range(32):
                    if s % 8 == 0 and s:
                        evac(D_A + s // 8 - 1, i, "copy")
                    if s in Q_AT:
                        gdn_read_act(i, Q_AT[s])
                evac(D_A + 3, i, "z")

            def attention_act(i, s):
                for m in range(16):
                    e, qt = divmod(m, NT)
                    w = min(BAND, qt + 1) * P
                    if s == SC_AT[m + 1] + 1:
                        act.wait_ge(pv_mm, i * 16 + m + 1)
                        if m == 0:
                            act.wait_ge(ya_free, i + LEAD)
                        act.activation(yast[e * A_D:(e + 1) * A_D, qt * P:(qt + 1) * P], aT[0:A_D, 0:P],
                                       ACT.Copy).then_inc(pv_read, 1)
                    if s == SC_AT[m + 1]:
                        act.wait_ge(at_mm, i * 18 + at_index(m=m) + 1)
                        ins = act.activation(PT[:, 0:min(w, 512)], aT[:, 0:min(w, 512)], ACT.Copy)
                        if w > 512:
                            ins = act.activation(PT[:, 512:w], fifth(s), ACT.Copy)
                        ins.then_inc(at_read, 1)
                for e in range(2):
                    if s == VT_AT[e]:
                        act.wait_ge(at_mm, i * 18 + at_index(e=e) + 1)
                        act.activation(V[:, e].rearrange("p a b -> p (a b)"), aT[:, :], ACT.Copy)\
                            .then_inc(at_read, 1)

            def exp_act(i, s):
                for m in range(16):
                    if s == SC_AT[m]:
                        w = min(BAND, m % NT + 1) * P
                        act.wait_ge(negm_ready, i * 16 + m + 1)
                        act.activation(Pm[:, 0:w], aS[:, 0:w], ACT.Exp, scale=SCALE, bias=negm[:, m % 2:m % 2 + 1],
                                       accum_out=psm[:, m % 2:m % 2 + 1]).then_inc(exp_ready, 1)

            with act.Fori(0, 4) as i:
                for s in range(32):
                    attention_act(i, s)
                    if s in Q_AT:
                        gdn_read_act(i + 4, Q_AT[s])
                    exp_act(i, s)
                    if s % 8 == 0 and s:
                        evac(D_B + s // 8 - 1, i, "tanh")
                attention_act(i, 32)
                evac(D_B + 3, i, "tanh")
            gdn_read_act(NT, Q_TO, 0)
            def squares(norm, b):
                if b >= 3:
                    act.wait_ge(sqs_ready, 6 * norm + b - 2)
                act.activation(tmp[:, :] if b == 0 else est[:, b % 2, :], xT[:, b, :], ACT.Square)\
                    .then_inc(sq_ready, 1)

            for k in range(8):
                act.wait_ge(y_in[k % 4], 16 * (k // 4 + 1))
                if k >= 4:
                    act.wait_ge(yz_ready, k - 3)
                act.activation(y_hi[:, k, :], yst[:, (k + 1) % 4, :], ACT.Copy).then_inc(yhi_ready, 1)
            for b in range(8):
                split_hi(D_M + b + 2)
                act.wait_ge(merged_ready, b + 1)
                act.activation(act_hi[:, b, :], est[:, b % 2, :], ACT.Copy).then_inc(mhi_ready, 1)
            for b in range(8):
                split_hi(D_O + b + 2)
                act.wait_ge(x2_ready, b + 1)
                squares(0, b)
            for k in range(KT):
                act.wait_ge(xn_ready, KT + k + 1)
                act.activation(act_hi[:, k, :], est[:, k % 2, :], ACT.Identity,
                               bias=modT[:, SH2 + k:SH2 + k + 1]).then_inc(hi_ready, 1)

            def ffn_hidden(n, i, ahead=True):
                ds = D_F + 2 * n
                act.wait_ge(dense_mm, ds + 1 + 8 * i)
                if ahead:
                    split_hi(ds + 2, 2 * i)
                act.wait_ge(gu_read, n + 4 * i)
                act.activation(est[:, 0, :], pm[2 if n == 1 else 0][:, :], ACT.Tanh, scale=0.5)\
                    .then_inc(gth_ready, 1)
                if ahead:
                    split_hi(ds + 3, 2 * i)
                act.wait_ge(gu_read, n + 1 + 4 * i)
                act.activation(h_hi[:, (n // 2) % 2, n % 2, :], est[:, 1, :], ACT.Copy).then_inc(hhi_ready, 1)

            def split_o(p, i):
                for e in range(2):
                    act.wait_ge(o_in[e], 16 * (p + 1) + 32 * i)
                    act.wait_ge(o_mm, 8 * p + 16 * i + LEAD)
                    act.activation(o_hi[:, e, :], f_raw[:, e, :], ACT.Copy).then_inc(ohi_ready, 1)

            ffn_hidden(0, 0)
            ffn_hidden(1, 0)

            def ffn_body(n, i, ahead=True):
                split_o(n - 1, i)
                ffn_hidden(2 * n, i)
                ffn_hidden(2 * n + 1, i, ahead)

            ffn_body(1, 0)
            with act.Fori(0, 4) as it:
                ffn_body(2, it)
                ffn_body(3, it)
            ffn_body(10, 0, ahead=False)
            split_o(10, 0)
            for b in range(8):
                act.wait_ge(po_free, 8 * 10 + b + 3)
                squares(1, b)

        @block.vector
        def _(dve):
            dve.sem_inc(bias_free, LEAD)
            dve.sem_inc(asc_ready, 2)
            ch = Chain(dve, vec_chain)

            def split_lo(ds, i=0):
                dve.wait_ge(whi_ready, ds + 1 + 4 * i)
                dve.tensor_tensor(w_lo[:, ds % 2], w_raw[:, ds % NR], w_hi[:, ds % 2].bitcast(F32), ALU.subtract)\
                    .then_inc(wlo_ready, 1)

            dve.wait_ge(act_chain, 1)
            ch.link(dve.scalar_tensor_tensor(cs[:, :], cth[:, :], 1.0, vT[:, V_C:V_C + 8], ALU.add, ALU.mult))
            ch.link(dve.tensor_scalar(cs[:, :], cs[:, :], 0.5, None, ALU.mult))
            dve.wait_ge(vec_chain, ch.n)
            dve.sem_inc(cs_ready, 1)

            def evac_x(t):
                dve.wait_ge(xt_mm, t + 1)
                dve.tensor_copy(xT0[:, :, t * P:(t + 1) * P], ps[t % 2][:, :].rearrange("p (k q) -> p k q", k=KT))\
                    .then_inc(xt_read, 1)

            def ada_sum(n):
                dve.wait_ge(ada_in[n % 2], 32 * (n // 2 + 1))
                dst = asum[:, n % 2, :]
                ch.link(dve.tensor_scalar(dst, adab[:, n % 2, 0, :], cs[:, 0:1], None, ALU.mult))
                for k in range(1, 5):
                    ins = dve.scalar_tensor_tensor(dst, adab[:, n % 2, k, :], cs[:, k:k + 1], dst,
                                                   ALU.mult, ALU.add)
                    if k < 4:
                        ch.link(ins)
                ins.then_inc(asum_ready, 1)

            for t in range(NT):
                evac_x(t)
            dve.wait_ge(ss_ready, NT)
            ch.link(dve.tensor_scalar(ss[:, :], ss[:, :], 1.0 / D, EPS, ALU.mult, ALU.add))
            rsqrt(ch, dve, ss[:, :], rr[:, :], rt[:, :])
            dve.wait_ge(consts_ready, 3)
            dve.tensor_tensor(dg0, bc_mid(ident[:, :], NT), bc(rr[:, :], P), ALU.mult).then_inc(diag_ready, 1)
            dve.wait_ge(xt_read, NT)
            ada_sum(0)
            split_lo(0)
            split_lo(1)

            def norm_scale(k, x_t, gain, rb, n0):
                if k >= 2:
                    dve.wait_ge(lo_ready, n0 + k - 1)
                dve.scalar_tensor_tensor(est[:, k % 2, :], x_t, gain, rb, ALU.mult, ALU.mult).then_inc(xn_ready, 1)

            def norm_lo(k, sh, n0):
                dve.wait_ge(hi_ready, n0 + k + 1)
                dve.scalar_tensor_tensor(act_lo[:, k, :], est[:, k % 2, :], modT[:, sh + k:sh + k + 1],
                                         act_hi[:, k, :].bitcast(F32), ALU.add, ALU.subtract).then_inc(lo_ready, 1)

            def both(v):
                return v.rearrange("p (a k) -> p a k", a=2)

            for n in range(4):
                if n < 3:
                    ada_sum(n + 1)
                dve.wait_ge(mod_mm, n + 1)
                two = slice(2 * n, 2 * n + 2)
                dve.tensor_tensor(both(modT[:, 0:16])[:, :, two], both(gps[:, 0:16])[:, :, two],
                                  both(vT[:, V_ADA:V_ADA + 16])[:, :, two], ALU.add).then_inc(mod_ready, 1)
                dve.wait_ge(mod_ready, n + 1)
                ch.link(dve.scalar_tensor_tensor(gs[:, two], modT[:, SC1 + 2 * n:SC1 + 2 * n + 2], 1.0,
                                                 vT[:, V_N1 + 2 * n:V_N1 + 2 * n + 2], ALU.add, ALU.mult))
                if n == 0:
                    dve.wait_ge(rb_mm, 1)
                for k in (2 * n, 2 * n + 1):
                    norm_scale(k, xT0[:, k, :], gs[:, k:k + 1], aS[:, :], 0)
                for k in (2 * n, 2 * n + 1):
                    norm_lo(k, SH1, 0)

            def conv(ds, i, taps):
                split_lo(ds + 2, i)
                dve.wait_ge(tap_ready, ds + 4 * i)
                e, q = est[:, ds % 2, :], ps[ds % 2]
                for s, w in zip((1, 2, 3), taps):
                    ins = dve.scalar_tensor_tensor(e[:, s:], q[:, 0:S - s], w, e[:, s:], ALU.mult, ALU.add)
                    if s < 3:
                        ch.link(ins)
                ins.then_inc(taps_ready, 1)
                dve.wait_ge(th_ready, ds + 4 * i)
                dve.scalar_tensor_tensor(e, tmp[:, :], 1.0, e, ALU.add, ALU.mult).then_inc(est_ready, 1)

            for d in range(D_CONV):
                if d == 0:
                    split_lo(2)
                    continue
                conv(d, 0, [wcT[:, (3 - s) * 12 + d - 1:(3 - s) * 12 + d] for s in (1, 2, 3)])
                if d == 2:
                    dve.wait_ge(abT_mm, 1)
                    dve.wait_ge(misc_in, 32)
                    ch.link(dve.tensor_copy(ab[:, :, :], gps[:, 0:64].rearrange("p (t h) -> p t h", t=NT)))
                    ch.link(dve.tensor_tensor(ab[:, :, 4:8], ab[:, :, 4:8], bc_mid(dtb[:, :], NT), ALU.add))
                    ch.link(dve.tensor_scalar(ab2[:, :, :], ab[:, :, :], -1.0, None, ALU.mult))
                    dve.tensor_tensor(eab[:, :, :], ab[:, :, :], ab2[:, :, :], ALU.max).then_inc(ab_abs, 1)
                if d == 3:
                    dve.wait_ge(ab_exp, 1)
                    eb, ea = eab[:, :, 0:4], eab[:, :, 4:8]
                    ch.link(dve.tensor_scalar(u1[:, :, :], ab[:, :, 0:4], 0.0, None, ALU.is_ge))
                    ch.link(dve.tensor_scalar(u2[:, :, :], eb, -1.0, 1.0, ALU.mult, ALU.add))
                    ch.link(dve.tensor_tensor(u1[:, :, :], u1[:, :, :], u2[:, :, :], ALU.mult))
                    ch.link(dve.tensor_tensor(u1[:, :, :], u1[:, :, :], eb, ALU.add))
                    ch.link(dve.tensor_scalar(u2[:, :, :], eb, 1.0, None, ALU.add))
                    ch.link(dve.reciprocal(u2[:, :, :], u2[:, :, :]))
                    ch.link(dve.tensor_tensor(beta[:, :, :], u1[:, :, :], u2[:, :, :], ALU.mult))
                    ch.link(dve.tensor_scalar(u1[:, :, :], ea, 2.0, None, ALU.add))
                    ch.link(dve.reciprocal(u1[:, :, :], u1[:, :, :]))
                    ch.link(dve.tensor_tensor(u1[:, :, :], u1[:, :, :], ea, ALU.mult))
                    ch.link(dve.tensor_tensor(u2[:, :, :], u1[:, :, :], u1[:, :, :], ALU.mult))
                    ch.link(dve.tensor_scalar(u3[:, :, :], u2[:, :, :], 1.0 / 15, None, ALU.mult))
                    for n in (13, 11, 9, 7, 5, 3):
                        ch.link(dve.scalar_tensor_tensor(u3[:, :, :], u3[:, :, :], 1.0 / n, u2[:, :, :],
                                                         ALU.add, ALU.mult))
                    ch.link(dve.scalar_tensor_tensor(u3[:, :, :], u3[:, :, :], 1.0, u1[:, :, :],
                                                     ALU.add, ALU.mult))
                    ch.link(dve.tensor_scalar(u2[:, :, :], ab[:, :, 4:8], 0.0, None, ALU.max))
                    ch.link(dve.scalar_tensor_tensor(u3[:, :, :], u3[:, :, :], 2.0, u2[:, :, :],
                                                     ALU.mult, ALU.add))
                    dve.wait_ge(act_chain, 3)
                    ch.link(dve.tensor_tensor(u3[:, :, :], u3[:, :, :], bc_mid(negA[:, :], NT), ALU.mult))
                    dve.tensor_scalar(g[:, :, :], u3[:, :, :], -1.0, None, ALU.mult).then_inc(g_ready, 1)
            base = ch.n
            with dve.Fori(0, 2) as i:
                ch = Chain(dve, vec_chain, i * 8 + base)
                for j in range(4):
                    ds = D_CONV + j
                    conv(ds, i, [wcT[:, bass.ds(i * 4 + (3 - s) * 12 + ds - 1, 1)] for s in (1, 2, 3)])
                assert ch.n == 8
            base += 16
            dve.wait_ge(eg_ready, 1)
            dve.tensor_scalar(neg_egc[:, :, :], eg[:, 0], -1.0, None, ALU.mult).then_inc(neg_ready, 1)
            dve.wait_ge(neg_ready, 1)

            def by_head(t3, t):
                return t3[:, bass.ds(t, 1), :].rearrange("p a h -> p (a h)")

            def gdn_dve(t, q):
                done = t * NQ + q + 1
                lv = part = None
                if Q_L1 <= q < Q_Y:
                    lv, part = level_of(q)
                if q == Q_D:
                    dve.wait_ge(ssk_ready, t * 4 + 4)
                    ch.link(dve.tensor_scalar(vkq[:, :], sskq[:, :], EPS, None, ALU.add))
                    ch.link(dve.reciprocal(cr[:, :], vkq[:, 0:4]))
                    dve.tensor_tensor(cj[:, :], cr[:, :], by_head(beta, t), ALU.mult).then_inc(cj_ready, 1)
                    dve.wait_ge(cj_ready, t + 1)
                    dve.tensor_tensor(cr[:, :], cj[:, :], by_head(eg[:, 1], t), ALU.mult).then_inc(cr_ready, 1)
                    rsqrt(ch, dve, vkq[:, :], rkq[:, :], tkq[:, :])
                    ch.link(dve.tensor_scalar(rq[:, :], rkq[:, 4:8], B_D ** -0.5, None, ALU.mult))
                    dve.tensor_tensor(nk[:, :], vkq[:, 0:4], rkq[:, 0:4], ALU.mult).then_inc(nk_ready, 1)
                if q == Q_QS:
                    dve.wait_ge(gdn_mm, done + LEAD)
                    dve.tensor_tensor(heads(om[:, :]), heads(gps[:, :]), bc(by_head(eg[:, 0], t), P), ALU.mult)\
                        .then_inc(gdn_read, 1)
                if q in (Q_GK, Q_GQ):
                    dve.wait_ge(gdn_mm, done + LEAD)
                    dve.wait_ge(ec_ready, t + 1)
                    dve.tensor_tensor((Lt if q == Q_GK else At)[:, :], gps[:, :], Ec[:, :], ALU.mult)\
                        .then_inc(gdn_read, 1)
                if q == Q_KS:
                    dve.wait_ge(gdn_mm, done + LEAD)
                    dve.tensor_tensor(heads(Xm[:, :]), heads(gps[:, :]), bc(by_head(neg_egc, t), P), ALU.mult)\
                        .then_inc(gdn_read, 1)
                if q == Q_TV:
                    dve.wait_ge(ct_ready, t * LEVELS + 1)
                    dve.tensor_tensor(heads(Um[:, :]), bc_mid(ident[:, :], B_H), heads(Ct[:, 0, :]),
                                      ALU.subtract).then_inc(u0_ready, 1)
                if part == 1:
                    dve.wait_ge(gdn_mm, done + LEAD)
                    dve.tensor_tensor(Tm[:, :], Tm[:, :], gps[:, :], ALU.subtract).then_inc(gdn_read, 1)
                if part == 2 and lv == LEVELS - 1:
                    dve.wait_ge(gdn_mm, done + LEAD)
                    dve.tensor_tensor(Um[:, :], Um[:, :], gps[:, :], ALU.subtract).then_inc(gdn_read, 1)
                if q == Q_AY:
                    dve.wait_ge(gdn_mm, done + LEAD)
                    dve.tensor_tensor(om[:, :], om[:, :], gps[:, :], ALU.add).then_inc(gdn_read, 1)
                if q == Q_KY:
                    dve.wait_ge(gdn_mm, done + LEAD)
                    for h in range(B_H):
                        ins = dve.scalar_tensor_tensor(hd(St, h), hd(St, h), by_head(eg[:, 2], t)[:, h:h + 1],
                                                       hd(gps, h), ALU.mult, ALU.add)
                    ins.then_inc(gdn_read, 1)

            def gdn_out(t):
                dve.wait_ge(sso_ready, t * 4 + 4)
                ch.link(dve.tensor_tensor(vo[:, :], sso[:, :], rq[:, :], ALU.mult))
                ch.link(dve.tensor_tensor(vo[:, :], vo[:, :], rq[:, :], ALU.mult))
                ch.link(dve.tensor_scalar(vo[:, :], vo[:, :], 1.0 / B_D, EPS, ALU.mult, ALU.add))
                rsqrt(ch, dve, vo[:, :], ro[:, :], to[:, :])
                ch.link(dve.tensor_tensor(ro[:, :], ro[:, :], rq[:, :], ALU.mult))
                dve.tensor_tensor(heads(on[:, :]), heads(om[:, :]), bc(ro[:, :], P), ALU.mult).then_inc(on_ready, 1)

            def ada_unit(i, a):
                dve.wait_ge(a_in[a % 2], i * (16 * ADA_PER // 2) + 16 * (a // 2 + 1))
                ch.link(dve.tensor_tensor(a_raw[:, a % 2], a_raw[:, a % 2], bc(cs[:, :], P), ALU.mult))
                dve.wait_ge(adam_mm, i * ADA_PER + max(a - 1, 0) + LEAD)
                dve.tensor_reduce(asc[:, a % 2, :], a_raw[:, a % 2].rearrange("p k c -> p c k"), AX_X, ALU.add)\
                    .then_inc(asc_ready, 1)

            LINKS_GDN = 2 + RSQRT_LINKS + 1 + 4 + RSQRT_LINKS
            LINKS_A = LINKS_GDN + ADA_PER
            with dve.Fori(0, 4) as i:
                ch = Chain(dve, vec_chain, i * LINKS_A + base)
                for s in range(32):
                    if s in Q_AT:
                        gdn_dve(i, Q_AT[s])
                    if s % 8 == 0 and s:
                        split_lo(D_A + s // 8 + 1, i)
                    if s % 4 == 1:
                        ada_unit(i, s // 4)
                gdn_out(i)
                dve.wait_ge(th_ready, i + 13)
                dve.wait_ge(est_stored[(D_A + 3) % 2], 16 * ((D_A + 2) // 2) + 32 * i)
                dve.scalar_tensor_tensor(est[:, (D_A + 3) % 2, :], tmp[:, :], 1.0, ps[(D_A + 3) % 2][:, :],
                                         ALU.add, ALU.mult).then_inc(est_ready, 1)
                split_lo(D_A + 5, i)
                assert ch.n == LINKS_A, ch.n
            base += 4 * LINKS_A
            ch = Chain(dve, vec_chain, base)
            dve.wait_ge(adam_mm, 4 * ADA_PER + LEAD)
            dve.tensor_tensor(modT[:, 16:48], aS[:, 0:32], vT[:, V_ADA + 16:V_ADA + 48], ALU.add).then_inc(ada_all, 1)
            dve.wait_ge(ada_all, 1)
            ch.link(dve.scalar_tensor_tensor(gs2[:, :], modT[:, SC2:SC2 + 8], 1.0, vT[:, V_N2:V_N2 + 8],
                                             ALU.add, ALU.mult))
            ch.link(dve.tensor_scalar(gt1h[:, :], modT[:, GT1:GT1 + 8], 0.5, None, ALU.mult))
            ch.link(dve.tensor_scalar(gt2h[:, :], modT[:, GT2:GT2 + 8], 0.5, None, ALU.mult))
            base += ch.n

            def scores_dve(i, m):
                e, qt = divmod(m, NT)
                w = min(BAND, qt + 1) * P
                dve.wait_ge(sc_mm, i * 16 + m + 1)
                near = aS[:, max(w - 2 * P, 0):w]
                ins = dve.tensor_tensor(near, near, bias[:, e, 2 * P - min(w, 2 * P):2 * P], ALU.add)
                if m == 15:
                    ins.then_inc(bias_free, 1)
                    dve.wait_ge(bias_free, i + 1 + LEAD)
                else:
                    ch.link(ins)
                if w == BAND * P:
                    ch.link(dve.memset(aS[A_D:P, 0:A_D], NEG))
                ch.link(dve.tensor_reduce(mx[:, m % 2:m % 2 + 1], aS[:, 0:w], AX_X, ALU.max))
                dve.tensor_scalar(negm[:, m % 2:m % 2 + 1], mx[:, m % 2:m % 2 + 1], -SCALE, None, ALU.mult)\
                    .then_inc(negm_ready, 1)

            def normalise(i, m):
                w = min(BAND, m % NT + 1) * P
                dve.wait_ge(exp_ready, i * 16 + m + 1 + LEAD)
                ch.link(dve.reciprocal(rsm[:, m % 2:m % 2 + 1], psm[:, m % 2:m % 2 + 1]))
                dve.tensor_scalar(Pm[:, 0:w], Pm[:, 0:w], rsm[:, m % 2:m % 2 + 1], None, ALU.mult)\
                    .then_inc(pn_ready, 1)

            LINKS_B = LINKS_GDN + 1 + 16 + 8 + 16 + 15
            with dve.Fori(0, 4) as i:
                ch = Chain(dve, vec_chain, i * LINKS_B + base)
                dve.wait_ge(bias_in, i * 32 + 32)
                ch.link(dve.memset(bias[0:A_D, :, 3 * A_D:4 * A_D], NEG))
                for s in range(32):
                    for m in range(16):
                        if SC_AT[m] == s - 1:
                            normalise(i, m)
                    for m in range(16):
                        if SC_AT[m] == s:
                            scores_dve(i, m)
                    if s in Q_AT:
                        gdn_dve(i + 4, Q_AT[s])
                    if s % 8 == 0 and s:
                        split_lo(D_B + s // 8 + 1, i)
                gdn_out(i + 4)
                split_lo(D_B + 5, i)
                assert ch.n == LINKS_B, (ch.n, LINKS_B)
            base += 4 * LINKS_B
            ch = Chain(dve, vec_chain, base)
            dve.wait_ge(est_ready, D_M - 1)
            dve.wait_ge(pv_read, 64 + LEAD)
            dve.wait_ge(gdn_read, NT * NQ + 1 + LEAD)
            dve.sem_inc(pair_free, 2)
            def y_lo_part(k):
                dve.wait_ge(yhi_ready, k + 1)
                dve.tensor_tensor(y_lo[:, k, :], yst[:, (k + 1) % 4, :], y_hi[:, k, :].bitcast(F32), ALU.subtract)\
                    .then_inc(ylo_ready, 1)

            for k in range(9):
                if 4 <= k < 8:
                    dve.wait_ge(y_in[k % 4], 16 * (k // 4 + 1))
                    dve.wait_ge(z_in[k % 2], 16 * (k // 2 - 1))
                    y = yst[:, (k + 1) % 4, :]
                    dve.tensor_tensor(y, y, gst2[:, k % 2, :], ALU.mult).then_inc(yz_ready, 1)
                if k:
                    y_lo_part(k - 1)
            dve.wait_ge(est_stored[0], 16 * 22)
            dve.wait_ge(est_stored[1], 16 * 22)
            for b in range(8):
                split_lo(D_M + b + 2)
                e = est[:, b % 2, :]
                dve.wait_ge(gate_in, 32 * (b + 1))
                dve.wait_ge(dense_mm, D_M + b + 1)
                ch.link(dve.scalar_tensor_tensor(e, gst2[:, 0, :], 1.0, pm[2 * (b % 2)][:, :], ALU.add, ALU.mult))
                dve.scalar_tensor_tensor(tmp[:, :], gst2[:, 1, :], 1.0, pm[2 * (b % 2) + 1][:, :],
                                         ALU.add, ALU.mult).then_inc(pair_free, 1)
                dve.wait_ge(pair_free, b + 3)
                dve.tensor_tensor(e, e, tmp[:, :], ALU.add).then_inc(merged_ready, 1)
                dve.wait_ge(mhi_ready, b + 1)
                dve.tensor_tensor(act_lo[:, b, :], e, act_hi[:, b, :].bitcast(F32), ALU.subtract)\
                    .then_inc(mlo_ready, 1)
            def add_squares(norm, b):
                if 1 <= b <= 6:
                    dve.wait_ge(sq_ready, 8 * norm + b + 1)
                    if b > 1:
                        dve.wait_ge(sqs_ready, 6 * norm + b - 1)
                    dve.tensor_tensor(tmp[:, :], tmp[:, :], est[:, b % 2, :], ALU.add).then_inc(sqs_ready, 1)

            def token_rsqrt(norm):
                dve.wait_ge(ss2_mm, norm + 1)
                ch.link(dve.tensor_copy(rt[:, :], pm[0][:, 8:16]))
                dve.tensor_tensor(ss[:, :], pm[0][:, 0:8], rt[:, :], ALU.add).then_inc(ss_read, 1)
                dve.wait_ge(ss_read, norm + 1)
                ch.link(dve.tensor_scalar(ss[:, :], ss[:, :], 1.0 / D, EPS, ALU.mult, ALU.add))
                rsqrt(ch, dve, ss[:, :], rr[:, :], rt[:, :])

            dve.wait_ge(xT_in, 16)
            for b in range(8):
                split_lo(D_O + b + 2)
                add_squares(0, b - 1)
                dve.wait_ge(dense_mm, D_O + b + 1)
                dve.scalar_tensor_tensor(xT[:, b, :], pm[b % 4][:, :], gt1h[:, b:b + 1], xT[:, b, :],
                                         ALU.mult, ALU.add).then_inc(x2_ready, 1)
            token_rsqrt(0)
            dve.tensor_tensor(dg0, bc_mid(ident[:, :], NT), bc(rr[:, :], P), ALU.mult).then_inc(diag2_ready, 1)
            dve.wait_ge(rb2_mm, 1)
            for k in range(KT + 1):
                if k < KT:
                    norm_scale(k, xT[:, k, :], gs2[:, k:k + 1], pm[3][:, :], KT)
                if k:
                    norm_lo(k - 1, SH2, KT)
            dve.sem_inc(po_free, 2)

            def ffn_hidden(n, i, ahead=True, between=lambda: None):
                ds = D_F + 2 * n
                if ahead:
                    split_lo(ds + 2, 2 * i)
                dve.wait_ge(gth_ready, n + 1 + 4 * i)
                ch.link(dve.scalar_tensor_tensor(est[:, 0, :], est[:, 0, :], 1.0, pm[2 if n == 1 else 0][:, :],
                                                 ALU.add, ALU.mult))
                if ahead:
                    split_lo(ds + 3, 2 * i)
                dve.wait_ge(dense_mm, ds + 2 + 8 * i)
                if n >= 2:
                    dve.wait_ge(hhi_ready, n + 4 * i)
                dve.tensor_tensor(est[:, 1, :], est[:, 0, :], pm[3 if n == 1 else 1][:, :], ALU.mult)\
                    .then_inc(gu_read, 1)
                between()
                dve.wait_ge(hhi_ready, n + 1 + 4 * i)
                dve.tensor_tensor(h_lo[:, (n // 2) % 2, n % 2, :], est[:, 1, :],
                                  h_hi[:, (n // 2) % 2, n % 2, :].bitcast(F32), ALU.subtract)\
                    .then_inc(hlo_ready, 1)

            def split_o(p, i):
                for e in range(2):
                    dve.wait_ge(ohi_ready, 2 * p + e + 1 + 4 * i)
                    dve.tensor_tensor(o_lo[:, e, :], f_raw[:, e, :], o_hi[:, e, :].bitcast(F32), ALU.subtract)\
                        .then_inc(olo_ready, 1)

            def accumulate(p, i, bs):
                for b in bs:
                    if b == 0:
                        dve.wait_ge(po_free, 8 * p + 2 + 16 * i)
                    dve.wait_ge(o_mm, 8 * p + b + 1 + 16 * i + LEAD)
                    dve.scalar_tensor_tensor(xT[:, b, :], pm[2 + b % 2][:, :], gt2h[:, b:b + 1], xT[:, b, :],
                                             ALU.mult, ALU.add).then_inc(po_free, 1)

            def ffn_body(n, i, ahead=True):
                split_o(n - 1, i)
                ffn_hidden(2 * n, i, between=lambda: accumulate(n - 1, i, [0]))
                accumulate(n - 1, i, range(1, 4))
                ffn_hidden(2 * n + 1, i, ahead, between=lambda: accumulate(n - 1, i, [4]))
                accumulate(n - 1, i, range(5, 8))

            ffn_hidden(0, 0)
            ffn_hidden(1, 0)
            ffn_body(1, 0)
            base += ch.n
            with dve.Fori(0, 4) as it:
                ch = Chain(dve, vec_chain, it * 4 + base)
                ffn_body(2, it)
                ffn_body(3, it)
                assert ch.n == 4
            base += 16
            ch = Chain(dve, vec_chain, base)
            ffn_body(10, 0, ahead=False)
            split_o(10, 0)
            for b in range(8):
                add_squares(1, b - 1)
                accumulate(10, 0, [b])
            token_rsqrt(1)
            dve.wait_ge(gbc_in, 16)
            for t in range(NT):
                dve.wait_ge(ft_mm, t + 1)
                dve.scalar_tensor_tensor(frow[:, t, :], pm[(t + 1) % 4][:, :], rr[:, t:t + 1], gbc[:, :],
                                         ALU.mult, ALU.mult).then_inc(row_ready, 1)


_INS = ["x", "c", "w_ada", "b_ada", "norm1_g", "norm2_g", "w_in", "rel_table", "w_conv", "a_log", "dt_bias",
        "gdn_norm_g", "w_branch_a", "w_branch_b", "w_out", "w_ffn_in", "w_ffn_out", "final_g"]


def kernel(**inputs):
    import numpy as _np
    import concourse.bacc as _bacc
    from concourse.bass_utils import run_bass_kernel_spmd as _run

    nc = _bacc.Bacc("TRN2", target_bir_lowering=False, num_devices=1)
    arrays, args = {}, []
    for name in _INS:
        a = _np.asarray(inputs[name])
        if name != "final_g":
            a = a[0]
        if name == "rel_table":
            a = a[:, ::-1]
        a = _np.ascontiguousarray(a)
        arrays[f"in_{name}_dram"] = a
        args.append(nc.dram_tensor(f"in_{name}_dram", a.shape, mybir.dt.from_np(a.dtype), kind="ExternalInput").ap())
    args.append(nc.dram_tensor("out_0_dram", (S, D), F32, kind="ExternalOutput").ap())
    hybrid_layer(nc, *args)
    r = _run(nc, [arrays], core_ids=[0])
    return r.results[0]["out_0_dram"].reshape(1, S, D)
```
